# Optimizing a Trainium2 kernel written in Bass

```python
import jax
import jax.numpy as jnp
from jax import lax
import numpy as np

D_MODEL = 2048
BATCH = 1
SEQ = 256
DEPTH = 1

F32 = jnp.float32
CHUNK = 64
N_META = 16
N_MIXERS = 3
CONV_WIDTH = 31
MLA_HEADS = D_MODEL // 128
MLA_Q_LORA = D_MODEL // 4
MLA_KV_LORA = D_MODEL // 8
MLA_NOPE = 128
MLA_ROPE = 64
MLA_V = 128
ROPE_THETA = 10000.0
Q_BLOCK = 128
HGRN_HEAD_DIM = 128
HGRN_HEADS = D_MODEL // HGRN_HEAD_DIM
HGRN_BLOCK = 16
N_EXPERTS = 32
N_GROUPS = 4
EXPERTS_PER_GROUP = N_EXPERTS // N_GROUPS
TOP_K = 2
EXPERT_FF = D_MODEL // 4
MOE_BLOCK = 256
DEEPNORM_ALPHA = (2 * DEPTH) ** 0.25
DEEPNORM_BETA = (8 * DEPTH) ** -0.25
N_CONV_LAYERS = len(range(0, DEPTH, N_MIXERS))
N_MLA_LAYERS = len(range(1, DEPTH, N_MIXERS))
N_HGRN_LAYERS = len(range(2, DEPTH, N_MIXERS))
LN_EPS = 1e-5
RMS_EPS = 1e-6

kernel_name = 'hybrid_chunk_causal_conv_mla_hgrn2_moe'

def layer_norm(x, g, b):
    xf = x.astype(F32)
    mu = xf.mean(-1, keepdims=True)
    var = jnp.square(xf - mu).mean(-1, keepdims=True)
    return ((xf - mu) * lax.rsqrt(var + LN_EPS) * g.astype(F32) + b.astype(F32)).astype(x.dtype)

def rms_norm(x, g):
    xf = x.astype(F32)
    y = xf * lax.rsqrt(jnp.mean(jnp.square(xf), -1, keepdims=True) + RMS_EPS)
    return (y * g.astype(F32)).astype(x.dtype)

def chunk_index(pos):
    return jnp.where(pos < N_META, 0, 1 + (pos - N_META) // CHUNK)

def rope_tables(length):
    inv = ROPE_THETA ** (-jnp.arange(0, MLA_ROPE, 2, dtype=F32) / MLA_ROPE)
    ang = jnp.arange(length, dtype=F32)[:, None] * inv[None, :]
    return jnp.cos(ang), jnp.sin(ang)

def apply_rope(x, cos, sin):
    xf = x.astype(F32)
    x1, x2 = jnp.split(xf, 2, axis=-1)
    return jnp.concatenate([x1 * cos - x2 * sin, x2 * cos + x1 * sin], axis=-1).astype(x.dtype)

def conformer_conv(x, pw1_w, pw1_b, dw_w, dw_b, ln_g, ln_b, pw2_w, pw2_b):
    a, gate = jnp.split(x @ pw1_w + pw1_b, 2, axis=-1)
    u = a * jax.nn.sigmoid(gate)
    u = lax.conv_general_dilated(
        u, dw_w[:, None, :], window_strides=(1,), padding=[(CONV_WIDTH - 1, 0)],
        dimension_numbers=('NWC', 'WIO', 'NWC'), feature_group_count=u.shape[-1]) + dw_b
    u = jax.nn.silu(layer_norm(u, ln_g, ln_b))
    return u @ pw2_w + pw2_b

def mla_attention(x, key_chunk, cos, sin, wdq, q_norm_g, wuq, wdkv, kv_norm_g, wukv, wo):
    B, L, _ = x.shape
    cq = rms_norm(x @ wdq, q_norm_g)
    q = (cq @ wuq).reshape(B, L, MLA_HEADS, MLA_NOPE + MLA_ROPE)
    q_nope = q[..., :MLA_NOPE]
    q_rope = apply_rope(q[..., MLA_NOPE:], cos[:, None, :], sin[:, None, :])
    ckv = x @ wdkv
    c_kv = rms_norm(ckv[..., :MLA_KV_LORA], kv_norm_g)
    k_rope = apply_rope(ckv[..., MLA_KV_LORA:], cos, sin)
    kv = (c_kv @ wukv).reshape(B, L, MLA_HEADS, MLA_NOPE + MLA_V)
    k_nope = kv[..., :MLA_NOPE]
    v = kv[..., MLA_NOPE:]
    n_blk = -(-L // Q_BLOCK)
    lq = n_blk * Q_BLOCK

    def blocks(t):
        t = jnp.pad(t, ((0, 0), (0, lq - L), (0, 0), (0, 0)))
        return t.reshape(B, n_blk, Q_BLOCK, t.shape[2], t.shape[3]).swapaxes(0, 1)

    q_chunk = chunk_index(jnp.arange(lq)).reshape(n_blk, Q_BLOCK)
    scale = (MLA_NOPE + MLA_ROPE) ** -0.5

    def attend(args):
        qn, qr, qc = args
        s = jnp.einsum('bqhd,bkhd->bhqk', qn, k_nope) + jnp.einsum('bqhr,bkr->bhqk', qr, k_rope)
        s = s.astype(F32) * scale
        visible = key_chunk[None, :] <= qc[:, None]
        p = jax.nn.softmax(jnp.where(visible, s, -jnp.inf), axis=-1).astype(v.dtype)
        return jnp.einsum('bhqk,bkhd->bqhd', p, v)

    o = lax.map(attend, (blocks(q_nope), blocks(q_rope), q_chunk))
    o = o.swapaxes(0, 1).reshape(B, lq, MLA_HEADS * MLA_V)[:, :L]
    return o @ wo

def hgrn2(x, w_in, lb, norm_g, wo):
    B, L, D = x.shape
    q, fz, i, g = jnp.split(x @ w_in, 4, axis=-1)
    fz = fz.astype(F32)
    log_f = jnp.logaddexp(jnp.log(lb), jnp.log1p(-lb) + jax.nn.log_sigmoid(fz))
    k = (1.0 - lb) * jax.nn.sigmoid(-fz)
    n = L // HGRN_BLOCK
    c = HGRN_BLOCK

    def to_blocks(t):
        return t.astype(F32).reshape(B, n, c, HGRN_HEADS, HGRN_HEAD_DIM).transpose(1, 0, 3, 2, 4)

    qb, kb, ib = to_blocks(q), to_blocks(k), to_blocks(i)
    bb = jnp.cumsum(to_blocks(log_f), axis=3)
    tri = jnp.arange(c)[:, None] >= jnp.arange(c)[None, :]

    def step(S, inp):
        qc, kc, ic, bc = inp
        o_inter = jnp.einsum('bhtd,bhde->bhte', qc * jnp.exp(bc), S)
        diff = bc[:, :, :, None, :] - bc[:, :, None, :, :]
        decay = jnp.exp(jnp.where(tri[:, :, None], diff, -jnp.inf))
        scores = jnp.einsum('bhtd,bhsd,bhtsd->bhts', qc, kc, decay)
        o = o_inter + jnp.einsum('bhts,bhse->bhte', scores, ic)
        b_last = bc[:, :, -1:, :]
        S = jnp.exp(b_last[:, :, 0, :, None]) * S + jnp.einsum('bhsd,bhse->bhde', kc * jnp.exp(b_last - bc), ic)
        return S, o

    s0 = jnp.zeros((B, HGRN_HEADS, HGRN_HEAD_DIM, HGRN_HEAD_DIM), F32)
    _, o = lax.scan(step, s0, (qb, kb, ib, bb))
    o = o.transpose(1, 0, 3, 2, 4).reshape(B, L, HGRN_HEADS, HGRN_HEAD_DIM)
    o = rms_norm(o, norm_g) * jax.nn.silu(g.astype(F32).reshape(B, L, HGRN_HEADS, HGRN_HEAD_DIM))
    return o.reshape(B, L, D).astype(x.dtype) @ wo

def moe_ffn(h, router_w, router_b, w_gate, w_up, w_down):
    T, D = h.shape
    scores = jax.nn.sigmoid(h.astype(F32) @ router_w.astype(F32))
    sel = (scores + router_b.astype(F32)).reshape(T, N_GROUPS, EXPERTS_PER_GROUP)
    group_score = lax.top_k(sel, 2)[0].sum(-1)
    g_top = jnp.argmax(group_score, axis=-1).astype(jnp.int32)
    in_group = sel[jnp.arange(T), g_top]
    _, local = lax.top_k(in_group, TOP_K)
    expert_idx = (g_top[:, None] * EXPERTS_PER_GROUP + local).astype(jnp.int32)
    gate = jnp.take_along_axis(scores, expert_idx, axis=1)
    gate = gate / gate.sum(-1, keepdims=True)
    n_assign = T * TOP_K
    flat_e = expert_idx.reshape(n_assign)
    flat_tok = jnp.repeat(jnp.arange(T, dtype=jnp.int32), TOP_K)
    order = jnp.argsort(flat_e)
    se, stok, sgate = flat_e[order], flat_tok[order], gate.reshape(n_assign)[order]
    counts = jnp.bincount(flat_e, length=N_EXPERTS)
    starts = jnp.cumsum(counts) - counts
    padded = (counts + MOE_BLOCK - 1) // MOE_BLOCK * MOE_BLOCK
    pends = jnp.cumsum(padded)
    pstarts = pends - padded
    dest = pstarts[se] + jnp.arange(n_assign, dtype=jnp.int32) - starts[se]
    n_blocks = -(-n_assign // MOE_BLOCK) + N_EXPERTS
    slot_tok = jnp.full((n_blocks * MOE_BLOCK,), T, jnp.int32).at[dest].set(stok)
    h_pad = jnp.concatenate([h, jnp.zeros((1, D), h.dtype)], axis=0)
    xb = h_pad[slot_tok].reshape(n_blocks, MOE_BLOCK, D)
    block_start = jnp.arange(n_blocks, dtype=jnp.int32) * MOE_BLOCK
    block_expert = jnp.minimum(jnp.searchsorted(pends, block_start, side='right'), N_EXPERTS - 1)

    def expert_block(args):
        xblk, e = args
        return (jax.nn.silu(xblk @ w_gate[e]) * (xblk @ w_up[e])) @ w_down[e]

    yb = lax.map(expert_block, (xb, block_expert)).reshape(n_blocks * MOE_BLOCK, D)
    return jnp.zeros((T, D), h.dtype).at[stok].add(yb[dest] * sgate[:, None].astype(h.dtype))

def setup_inputs(seed: int = 0) -> dict:
    key = jax.random.key(seed)
    k = jax.random.split(key, 32)

    def dense(kk, shape, fan_in, scale=1.0):
        return jax.random.normal(kk, shape, F32) * (scale * fan_in ** -0.5)

    def gain(kk, shape):
        return 1.0 + 0.02 * jax.random.normal(kk, shape, F32)

    def small(kk, shape, s=0.02):
        return s * jax.random.normal(kk, shape, F32)

    qk_dim = MLA_NOPE + MLA_ROPE
    ukv_scale = jnp.tile(jnp.concatenate([jnp.ones((MLA_NOPE,), F32), jnp.full((MLA_V,), DEEPNORM_BETA, F32)]), MLA_HEADS)
    hin_scale = jnp.concatenate([jnp.ones((2 * D_MODEL,), F32), jnp.full((D_MODEL,), DEEPNORM_BETA, F32), jnp.ones((D_MODEL,), F32)])
    return {
        'x': jax.random.normal(k[0], (BATCH, SEQ, D_MODEL), F32),
        'meta_tokens': jax.random.normal(k[1], (N_META, D_MODEL), F32),
        'ln_mix_g': gain(k[2], (DEPTH, D_MODEL)),
        'ln_mix_b': small(k[3], (DEPTH, D_MODEL)),
        'ln_ffn_g': gain(k[4], (DEPTH, D_MODEL)),
        'ln_ffn_b': small(k[5], (DEPTH, D_MODEL)),
        'conv_pw1_w': dense(k[6], (N_CONV_LAYERS, D_MODEL, 2 * D_MODEL), D_MODEL),
        'conv_pw1_b': small(k[7], (N_CONV_LAYERS, 2 * D_MODEL)),
        'conv_dw_w': dense(k[8], (N_CONV_LAYERS, CONV_WIDTH, D_MODEL), CONV_WIDTH),
        'conv_dw_b': small(k[9], (N_CONV_LAYERS, D_MODEL)),
        'conv_ln_g': gain(k[10], (N_CONV_LAYERS, D_MODEL)),
        'conv_ln_b': small(k[11], (N_CONV_LAYERS, D_MODEL)),
        'conv_pw2_w': dense(k[12], (N_CONV_LAYERS, D_MODEL, D_MODEL), D_MODEL, DEEPNORM_BETA),
        'conv_pw2_b': small(k[13], (N_CONV_LAYERS, D_MODEL)),
        'mla_wdq': dense(k[14], (N_MLA_LAYERS, D_MODEL, MLA_Q_LORA), D_MODEL),
        'mla_q_norm_g': gain(k[15], (N_MLA_LAYERS, MLA_Q_LORA)),
        'mla_wuq': dense(k[16], (N_MLA_LAYERS, MLA_Q_LORA, MLA_HEADS * qk_dim), MLA_Q_LORA),
        'mla_wdkv': dense(k[17], (N_MLA_LAYERS, D_MODEL, MLA_KV_LORA + MLA_ROPE), D_MODEL),
        'mla_kv_norm_g': gain(k[18], (N_MLA_LAYERS, MLA_KV_LORA)),
        'mla_wukv': dense(k[19], (N_MLA_LAYERS, MLA_KV_LORA, MLA_HEADS * (MLA_NOPE + MLA_V)), MLA_KV_LORA) * ukv_scale,
        'mla_wo': dense(k[20], (N_MLA_LAYERS, MLA_HEADS * MLA_V, D_MODEL), MLA_HEADS * MLA_V, DEEPNORM_BETA),
        'hgrn_w_in': dense(k[21], (N_HGRN_LAYERS, D_MODEL, 4 * D_MODEL), D_MODEL) * hin_scale,
        'hgrn_lb_logits': jax.random.normal(k[22], (DEPTH, D_MODEL), F32),
        'hgrn_norm_g': gain(k[23], (N_HGRN_LAYERS, HGRN_HEAD_DIM)),
        'hgrn_wo': dense(k[24], (N_HGRN_LAYERS, D_MODEL, D_MODEL), D_MODEL, DEEPNORM_BETA),
        'router_w': dense(k[25], (D_MODEL, N_EXPERTS), D_MODEL),
        'router_b': small(k[26], (N_EXPERTS,), 0.01),
        'moe_w_gate': dense(k[27], (DEPTH, N_EXPERTS, D_MODEL, EXPERT_FF), D_MODEL),
        'moe_w_up': dense(k[28], (DEPTH, N_EXPERTS, D_MODEL, EXPERT_FF), D_MODEL, DEEPNORM_BETA),
        'moe_w_down': dense(k[29], (DEPTH, N_EXPERTS, EXPERT_FF, D_MODEL), EXPERT_FF, DEEPNORM_BETA),
    }

def reference(x, meta_tokens, ln_mix_g, ln_mix_b, ln_ffn_g, ln_ffn_b,
              conv_pw1_w, conv_pw1_b, conv_dw_w, conv_dw_b, conv_ln_g, conv_ln_b, conv_pw2_w, conv_pw2_b,
              mla_wdq, mla_q_norm_g, mla_wuq, mla_wdkv, mla_kv_norm_g, mla_wukv, mla_wo,
              hgrn_w_in, hgrn_lb_logits, hgrn_norm_g, hgrn_wo,
              router_w, router_b, moe_w_gate, moe_w_up, moe_w_down):
    B = x.shape[0]
    meta = jnp.broadcast_to(meta_tokens[None].astype(x.dtype), (B, N_META, D_MODEL))
    h = jnp.concatenate([meta, x], axis=1)
    L = h.shape[1]
    key_chunk = chunk_index(jnp.arange(L))
    cos, sin = rope_tables(L)
    p_lb = jax.nn.softmax(hgrn_lb_logits.astype(F32), axis=0)
    lower_bounds = jnp.cumsum(p_lb, axis=0) - p_lb[0]
    for i in range(DEPTH):
        j = i // N_MIXERS
        kind = i % N_MIXERS
        if kind == 0:
            mix = conformer_conv(h, conv_pw1_w[j], conv_pw1_b[j], conv_dw_w[j], conv_dw_b[j],
                                 conv_ln_g[j], conv_ln_b[j], conv_pw2_w[j], conv_pw2_b[j])
        elif kind == 1:
            mix = mla_attention(h, key_chunk, cos, sin, mla_wdq[j], mla_q_norm_g[j], mla_wuq[j],
                                mla_wdkv[j], mla_kv_norm_g[j], mla_wukv[j], mla_wo[j])
        else:
            mix = hgrn2(h, hgrn_w_in[j], lower_bounds[i], hgrn_norm_g[j], hgrn_wo[j])
        h = layer_norm(DEEPNORM_ALPHA * h + mix, ln_mix_g[i], ln_mix_b[i])
        ffn = moe_ffn(h.reshape(B * L, D_MODEL), router_w, router_b,
                      moe_w_gate[i], moe_w_up[i], moe_w_down[i]).reshape(B, L, D_MODEL)
        h = layer_norm(DEEPNORM_ALPHA * h + ffn, ln_ffn_g[i], ln_ffn_b[i])
    return h[:, N_META:]


_drawn_inputs = setup_inputs


def setup_inputs(seed=0):
    import zlib

    import numpy as np

    out = dict(_drawn_inputs(seed))
    spreads = {}
    factors = {'ln_ffn_g': 8.135,
     'ln_ffn_b': 7.835,
     'conv_ln_g': 4.322,
     'conv_ln_b': 10.817,
     'conv_pw2_b': 3.723}
    for name, (base, spread) in spreads.items():
        noise = np.random.default_rng([zlib.crc32(name.encode()), seed]).standard_normal(out[name].shape)
        drawn = base * np.exp(spread * noise) if base else spread * noise
        out[name] = jnp.asarray(drawn.astype(out[name].dtype))
    for name, factor in factors.items():
        out[name] = (out[name] * factor).astype(out[name].dtype)
    return out
```

```python
import concourse.bass as bass
from concourse import mybir
from concourse.bass import ds
from contextlib import ExitStack

D = 2048
SEQ = 256
META = 16
LEN = META + SEQ
TAPS = 31
E = 32
GROUPS = 4
PER = E // GROUPS
FF = 512
P = 128
KT = D // P
TT = SEQ // P
SLOTS = 64
BLOCKS = SEQ // SLOTS
ALPHA = 2.0 ** 0.25
LN_EPS = 1e-5
PAD = TAPS - 1 - META
PAR = 5 + TAPS
RING = 12
CONV_SLOTS = 8
BIG = 4096.0
LOOKUPS = BLOCKS + 1
N_CONSTS = 11
TAP_OPS = 1 + 4 + 4 * TAPS


def build(nc, xT_in, x_in, par_in, w1, w2, b2, ln1_g, ln1_b, ln2_g, ln2_b, rw_in, rb_in, wg, wu, wd, out):
    f32, u32, i32 = mybir.dt.float32, mybir.dt.uint32, mybir.dt.int32
    ALU, ACT, AX = mybir.AluOpType, mybir.ActivationFunctionType, mybir.AxisListType

    ctx = ExitStack()
    with ctx:
        def sb(name, shape, dt=f32):
            return ctx.enter_context(nc.sbuf_tensor(name, shape, dt))

        def sem(name):
            return ctx.enter_context(nc.semaphore(name))

        h_rows = nc.dram_tensor("h_rows", (SEQ * 2, D // 2), f32, kind="Internal").ap()
        y_rows = nc.dram_tensor("y_rows", (SEQ * 2 * 2, D // 2), f32, kind="Internal").ap()

        ring = sb("ring", [P, RING, 2048])
        xT = sb("xT", [P, KT, LEN])
        squares = xT[:, :, 0:SEQ]
        hT = xT[:, :, 0:SEQ]
        conv = sb("conv", [P, KT, SEQ])
        h = sb("h", [P, TT, D])
        gain = sb("gain", [P, D])
        bias = sb("bias", [P, D])
        par = sb("par", [P, KT * PAR])
        par_now = sb("par_now", [P, 4 * PAR])
        glu_sig = sb("glu_sig", [P, 4, LEN])
        u = sb("u", [P, 4, PAD + LEN])
        acc = sb("acc", [P, 4, SEQ])
        mean_sb = sb("mean_sb", [P, SEQ])
        rstd_c = sb("rstd_c", [P, SEQ])
        b2_row = sb("b2_row", [1, D])
        ones = sb("ones", [P, P])
        mean_w = sb("mean_w", [P, P])
        ident = sb("ident", [P, P])
        before = sb("before", [P, P])
        rw = sb("rw", [P, KT * E])
        rb = sb("rb", [P, E])
        stats = sb("stats", [P, TT, 4, 6])
        mv = sb("mv", [P, TT, 2])
        rstd = sb("rstd", [P, TT])
        score = sb("score", [P, TT, E])
        sel = sb("sel", [P, TT, E])
        top8 = sb("top8", [P, TT, GROUPS, 8])
        gscore = sb("gscore", [P, TT, GROUPS])
        gbest = sb("gbest", [P, TT])
        gmark = sb("gmark", [P, TT, GROUPS])
        gfirst = sb("gfirst", [P, TT])
        grank = sb("grank", [P, GROUPS])
        sel_in = sb("sel_in", [P, TT, E])
        best = sb("best", [P, TT, 8])
        best_at = sb("best_at", [P, TT, 8], u32)
        best_f = sb("best_f", [P, TT, 2])
        hot = sb("hot", [P, 2, TT, E])
        gates = sb("gates", [P, 2, TT])
        gsum = sb("gsum", [P, TT])
        picked = sb("picked", [P, E])
        routed = sb("routed", [P, TT, E])
        rank = sb("rank", [P, TT, E])
        rows = sb("rows", [P, TT, E, 2])
        token2 = sb("token2", [P, TT])
        expert_no = sb("expert_no", [P, E])
        most = sb("most", [P, 1])
        more = sb("more", [P, BLOCKS])
        pairs_f = sb("pairs_f", [P, 1])
        pairs_i = sb("pairs_i", [P, 1], i32)
        slot_no = sb("slot_no", [P, LOOKUPS, 2, SLOTS])
        half_off = sb("half_off", [P, 1])
        pick = sb("pick", [P, 2, TT, P])
        g_at = [sb(f"g_at{q}", [P, 1], u32) for q in range(2)]
        s_at = [sb(f"s_at{q}", [P, 1], u32) for q in range(2)]
        xg = [sb(f"xg{q}", [P, 1024]) for q in range(2)]
        xgT = [conv[:, 4 * q:4 * q + 4, :].rearrange("p k (a c) -> p (k a) c", c=P) for q in range(2)]
        y = [conv[:, 8 + 4 * q:12 + 4 * q, :].rearrange("p k c -> p (k c)") for q in range(2)]
        act_sb, mid = acc[:, 0, :], acc[:, 1, :]
        midT = acc[:, 2, :].rearrange("p (c s) -> p c s", c=2)

        ps = ctx.enter_context(nc.psum_tensor("ps", [P, 8, 512], f32))
        ps_g, ps_u, ps_mid, ps_idx = ps[:, 0, 0:256], ps[:, 1, 0:256], ps[:, 2, 0:256], ps[:, 3, 0:2]
        ps_xT, ps_y = ps[:, 4:6, :], ps[:, 6:8, :]

        arrived = [sem(f"arrived{s}") for s in range(RING)]
        freed = [sem(f"freed{s}") for s in range(RING)]
        xT_in_s = [sem("xT_lo"), sem("xT_hi")]
        par_s, x_s, b2_s, gain_s, bias_s, rw_s, rb_s = (
            sem(n) for n in ("par_in", "x_in", "b2_in", "gain_in", "bias_in", "rw_in", "rb_in"))
        consts = sem("consts")
        marks = sem("marks")
        glu_s = sem("glu_s")
        taps = sem("taps")
        sums = sem("sums")
        centred = sem("centred")
        squared = sem("squared")
        var_in = sem("var_in")
        root = sem("root")
        scaled = sem("scaled")
        silu_c = sem("silu_c")
        pw2 = sem("pw2")
        step = sem("step")
        root1 = sem("root1")
        var1 = sem("var1")
        h_ready = sem("h_ready")
        h_stored = sem("h_stored")
        hT_ps = sem("hT_ps")
        hT_sb = sem("hT_sb")
        logits = sem("logits")
        scores_s = sem("scores")
        routed_s = sem("routed_s")
        ranks_ps = sem("ranks_ps")
        pairs_s = sem("pairs_s")
        alpha_h = sem("alpha_h")
        picked_s = sem("picked_s")
        idx_ps = sem("idx_ps")
        idx_sb = sem("idx_sb")
        gather_turn, scatter_turn = sem("gather_turn"), sem("scatter_turn")
        gathered = [sem(f"gathered{q}") for q in range(2)]
        scattered = [sem(f"scattered{q}") for q in range(2)]
        xT_ps = sem("xT_ps")
        xT_sb = sem("xT_sb")
        act_done = sem("act_done")
        mid_done = sem("mid_done")
        midT_ps = sem("midT_ps")
        midT_sb = sem("midT_sb")
        y_sb = [sem("y_sb_act"), sem("y_sb_dve")]
        experts_done = sem("experts_done")
        y_in = [sem(f"y_in{t}") for t in range(TT)]
        gain2_s, bias2_s = sem("gain2_in"), sem("bias2_in")
        var2, root2 = sem("var2"), sem("root2")
        out_ready = sem("out_ready")
        out_s = sem("out_s")

        block = ctx.enter_context(nc.Block())

        def wait(eng, s, value):
            if isinstance(value, int) and value <= 0:
                return
            eng.wait_ge(s, value)

        w1_v = w1.rearrange("(k p) n -> p k n", p=P)
        wg_v = wg.rearrange("e (g p c) n -> e g p (c n)", g=2, c=8)
        wu_v = wu.rearrange("e (g p c) n -> e g p (c n)", g=2, c=8)
        wd_v = wd.rearrange("e (f p) n -> e f p n", p=P)

        CHUNKS = []
        for g in range(2):
            for c0 in (0, 4):
                CHUNKS += [("gate", g, c0), ("up", g, c0)]
        CHUNKS += [("down", f, 0) for f in range(4)]

        def slot_of(j):
            return (CONV_SLOTS + j) % RING

        def used_before(s):
            return 8 * 4 // CONV_SLOTS + KT // CONV_SLOTS if s < CONV_SLOTS else 0

        def chunk_used(eng, j, items):
            if not (isinstance(items, int) and items <= 0):
                eng.wait_ge(freed[slot_of(j)], used_before(slot_of(j)) + items)

        GATE_END, UP_END, DOWN_END = 6, 7, 11

        def expert_of(m):
            return m % E

        def block_of(m):
            return m // E

        def item_loop(eng, body, more_pairs):
            body(0)
            with eng.Fori(1, E // 2) as i:
                body(i)
            with eng.If(more_pairs > E // 2):
                with eng.Fori(E // 2, more_pairs) as i:
                    body(i)

        def load_pairs(eng):
            eng.wait_ge(pairs_s, 1)
            return eng.value_load(pairs_i[0:1, 0:1], min_val=E // 2, max_val=BLOCKS * E // 2)

        @block.sync
        def _(sp):
            def pw1_chunks(i):
                for q in range(2):
                    for c in range(4):
                        s = 4 * q + c
                        col = (c // 2) * D + (2 * i + q) * 256
                        wait(sp, freed[s], i)
                        k0 = 8 * (c % 2)
                        sp.dma_start(ring[:, s, :].rearrange("p (k n) -> p k n", k=8),
                                     w1_v[:, k0:k0 + 8, ds(col, 256)]).then_inc(arrived[s], 16)

            sp.dma_start(par[:, :], par_in).then_inc(par_s, 16)
            for half in range(2):
                sp.dma_start(xT[:, 8 * half:8 * half + 8, :],
                             xT_in.rearrange("(k p) t -> p k t", p=P)[:, 8 * half:8 * half + 8, :]
                             ).then_inc(xT_in_s[half], 16)
            pw1_chunks(0)
            sp.dma_start(h[:, :, :], x_in.rearrange("(t p) d -> p t d", p=P)).then_inc(x_s, 16)
            sp.dma_start(b2_row[:, :], b2).then_inc(b2_s, 16)
            sp.dma_start(gain[:, :], ln1_g.broadcast_to([P, D])).then_inc(gain_s, 16)
            sp.dma_start(bias[:, :], ln1_b.broadcast_to([P, D])).then_inc(bias_s, 16)
            sp.dma_start(rw[:, :], rw_in).then_inc(rw_s, 16)
            sp.dma_start(rb[:, :], rb_in.broadcast_to([P, E])).then_inc(rb_s, 16)
            with sp.Fori(1, 4) as i:
                pw1_chunks(i)
            for k in range(KT):
                s = k % CONV_SLOTS
                sp.wait_ge(freed[s], 4 + k // CONV_SLOTS)
                sp.dma_start(ring[:, s, :], w2[k * P:(k + 1) * P, :]).then_inc(arrived[s], 16)

            def expert_chunks(n):
                e = expert_of(n)
                for j, (kind, a, c0) in enumerate(CHUNKS):
                    s = slot_of(j)
                    wait(sp, freed[s], used_before(s) + n)
                    if kind == "down":
                        src = wd_v[ds(e, 1), a, :, :].rearrange("o p n -> (o p) n")
                    else:
                        src = (wg_v if kind == "gate" else wu_v)[ds(e, 1), a, :, c0 * FF:(c0 + 4) * FF]\
                            .rearrange("o p n -> (o p) n")
                    sp.dma_start(ring[:, s, :], src).then_inc(arrived[s], 16)

            def pair(i):
                for q in range(2):
                    expert_chunks(2 * i + q)

            pair(0)
            sp.wait_ge(h_ready, TT)
            sp.dma_start(gain[:, :], ln2_g.broadcast_to([P, D])).then_inc(gain2_s, 16)
            sp.dma_start(bias[:, :], ln2_b.broadcast_to([P, D])).then_inc(bias2_s, 16)
            more_pairs = load_pairs(sp)
            with sp.Fori(1, E // 2) as i:
                pair(i)
            with sp.If(more_pairs > E // 2):
                with sp.Fori(E // 2, more_pairs) as i:
                    pair(i)

            sp.wait_ge(experts_done, 1)
            y_v = y_rows.rearrange("(t p c) d -> t p (c d)", t=TT, c=4)
            for t in range(TT):
                sp.dma_start(ring[:, 2 * t:2 * t + 2, :], y_v[t].rearrange("p (a n) -> p a n", a=2)
                             ).then_inc(y_in[t], 16)
            for t in range(TT):
                sp.wait_ge(out_ready, t + 1)
                sp.dma_start(out[t * P:(t + 1) * P, :], h[:, t, :]).then_inc(out_s, 16)
            sp.wait_ge(out_s, 16 * TT)

        @block.gpsimd
        def _(pool):
            n_marks = [0]

            def mark(ins):
                n_marks[0] += 1
                ins.then_inc(marks, 1)
                pool.wait_ge(marks, n_marks[0])

            def const(ins):
                ins.then_inc(consts, 1)

            const(nc.gpsimd.memset(ones[:, :], 1.0))
            const(nc.gpsimd.memset(mean_w[:, :], 1.0 / D))
            mark(nc.gpsimd.memset(ident[:, :], 0.0))
            const(nc.gpsimd.affine_select(out=ident[:, :], in_=ident[:, :], compare_op=ALU.not_equal, fill=1.0,
                                         base=0, pattern=[[-1, P]], channel_multiplier=1))
            mark(nc.gpsimd.memset(before[:, :], 0.0))
            const(nc.gpsimd.affine_select(out=before[:, :], in_=before[:, :], compare_op=ALU.is_ge, fill=1.0,
                                         base=0, pattern=[[-1, P]], channel_multiplier=1))
            fl = dict(allow_small_or_imprecise_dtypes=True)
            const(nc.gpsimd.iota(token2[:, :], [[2 * P, TT]], base=0, channel_multiplier=2, **fl))
            const(nc.gpsimd.iota(expert_no[:, :], [[1, E]], base=0, channel_multiplier=0, **fl))
            const(nc.gpsimd.iota(grank[:, :], [[-1, GROUPS]], base=GROUPS, channel_multiplier=0, **fl))
            const(nc.gpsimd.iota(slot_no[:, :, :, :], [[SLOTS, LOOKUPS], [0, 2], [1, SLOTS]], base=0,
                                 channel_multiplier=0, **fl))
            mark(nc.gpsimd.memset(half_off[:, :], BIG + 1.0))
            const(nc.gpsimd.affine_select(out=half_off[:, :], in_=half_off[:, :], compare_op=ALU.is_ge, fill=BIG,
                                          base=-SLOTS, pattern=[[0, 1]], channel_multiplier=1))
            for q in range(2):
                const(nc.gpsimd.memset(xg[q][:, :], 0.0))

            pool.wait_ge(consts, N_CONSTS)
            more_pairs = load_pairs(pool)
            pool.wait_ge(h_stored, 16 * TT)

            last_h, last_y = pool.to_reg(SEQ * 2 - 1), pool.to_reg(SEQ * 4 - 1)

            def gather(m, q):
                pool.wait_ge(idx_sb, m + 1)
                wait(pool, xT_ps, m - 1)
                pool.sem_inc(gather_turn, 1)
                nc.gpsimd.indirect_dma_start(
                    out=xg[q][:, :], out_offset=None, in_=h_rows,
                    in_offset=bass.IndirectOffsetOnAxis(ap=g_at[q][:, 0:1], axis=0),
                    bounds_check=last_h, oob_is_err=False).then_inc(gathered[q], 16)

            def pair(i):
                for q in range(2):
                    n = 2 * i + q
                    gather(n + 1, 1 - q)
                    pool.wait_ge(y_sb[0], n + 1)
                    pool.wait_ge(y_sb[1], n + 1)
                    pool.sem_inc(scatter_turn, 1)
                    nc.gpsimd.indirect_dma_start(
                        out=y_rows, out_offset=bass.IndirectOffsetOnAxis(ap=s_at[q][:, 0:1], axis=0),
                        in_=y[q][:, :], in_offset=None,
                        bounds_check=last_y, oob_is_err=False).then_inc(scattered[q], 16)

            gather(0, 0)
            pair(0)
            with pool.Fori(1, E // 2) as i:
                pair(i)
            for q in range(2):
                pool.wait_ge(scattered[q], 16 * (E // 2))
            pool.wait_ge(gathered[0], 16 * (E // 2 + 1))
            with pool.If(more_pairs > E // 2):
                with pool.Fori(E // 2, more_pairs) as i:
                    pair(i)
                for q in range(2):
                    pool.wait_ge(scattered[q], 16 * more_pairs)
                pool.wait_ge(gathered[0], 16 * more_pairs + 16)
            pool.sem_inc(experts_done, 1)

        @block.scalar
        def _(act):
            act.wait_ge(par_s, 16)

            def gates_of(i):
                for j in range(4):
                    q, c = j // 2, j % 2
                    act.wait_ge(freed[4 * q + 3], i + 1)
                    wait(act, taps, (i - 1) * TAP_OPS + 5)
                    nc.scalar.activation(glu_sig[:, j, :], ps[:, 4 * q + 2 + c, 0:LEN], ACT.Sigmoid,
                                         bias=par[:, ds((4 * i + j) * PAR + 1, 1)]).then_inc(glu_s, 1)

            gates_of(0)
            with act.Fori(1, 4) as i:
                gates_of(i)

            for c in range(4):
                act.wait_ge(centred, c + 1)
                nc.scalar.activation(squares[:, 4 * c:4 * c + 4, :], conv[:, 4 * c:4 * c + 4, :], ACT.Square
                                     ).then_inc(squared, 1)
            act.wait_ge(var_in, 1)
            nc.scalar.activation(rstd_c[:, :], rstd_c[:, :], ACT.Sqrt).then_inc(root, 1)
            for k in range(KT):
                act.wait_ge(scaled, k // 4 + 1)
                nc.scalar.activation(conv[:, k, :], conv[:, k, :], ACT.Silu,
                                     scale=par[:, k * PAR + 3:k * PAR + 4],
                                     bias=par[:, k * PAR + 4:k * PAR + 5]).then_inc(silu_c, 1)
            for t in range(TT):
                act.wait_ge(var1, t + 1)
                nc.scalar.activation(rstd[:, t:t + 1], rstd[:, t:t + 1], ACT.Sqrt).then_inc(root1, 1)
            h_store = h_rows.rearrange("(t p g) c -> t p (g c)", t=TT, g=2)
            for t in range(TT):
                act.wait_ge(h_ready, t + 1)
                act.dma_start(h_store[t], h[:, t, :]).then_inc(h_stored, 16)
                act.wait_ge(hT_ps, t + 1)
                nc.scalar.activation(hT[:, 0:8, t * P:(t + 1) * P],
                                     ps[:, 4 * t:4 * t + 2, :].rearrange("p b (k c) -> p (b k) c", c=P),
                                     ACT.Copy).then_inc(hT_sb, 1)
            act.wait_ge(logits, 1)
            nc.scalar.activation(score[:, :, :], ps[:, 0, 0:TT * E].rearrange("p (t e) -> p t e", t=TT),
                                 ACT.Sigmoid).then_inc(scores_s, 1)
            more_pairs = load_pairs(act)

            def evacuate_xT(m, q):
                act.wait_ge(xT_ps, m + 1)
                chunk_used(act, UP_END, m - 1)
                nc.scalar.activation(xgT[q][:, :, :], ps_xT.rearrange("p b (k c) -> p (b k) c", c=P),
                                     ACT.Copy).then_inc(xT_sb, 1)

            def pair(i):
                for q in range(2):
                    n = 2 * i + q
                    chunk_used(act, GATE_END, n + 1)
                    wait(act, mid_done, n)
                    nc.scalar.activation(act_sb, ps_g, ACT.Silu).then_inc(act_done, 1)
                    evacuate_xT(n + 1, 1 - q)
                    chunk_used(act, DOWN_END, n + 1)
                    wait(act, scattered[q], 16 * i)
                    nc.scalar.activation(y[q][:, 0:512], ps_y[:, 0, :], ACT.Copy).then_inc(y_sb[0], 1)

            evacuate_xT(0, 0)
            pair(0)
            with act.Fori(1, E // 2) as i:
                pair(i)
            with act.If(more_pairs > E // 2):
                with act.Fori(E // 2, more_pairs) as i:
                    pair(i)

            for t in range(TT):
                act.wait_ge(var2, t + 1)
                nc.scalar.activation(rstd[:, t:t + 1], rstd[:, t:t + 1], ACT.Sqrt).then_inc(root2, 1)

        @block.vector
        def _(dve):
            n_step = [0]

            def done(ins):
                n_step[0] += 1
                ins.then_inc(step, 1)
                dve.wait_ge(step, n_step[0])

            done(nc.vector.memset(u[:, :, 0:PAD], 0.0))
            dve.wait_ge(par_s, 16)

            def conv_pass(i):
                base = i * TAP_OPS
                wait(dve, taps, base)
                nc.vector.tensor_copy(par_now[:, :], par[:, ds(4 * i * PAR, 4 * PAR)]).then_inc(taps, 1)
                for j in range(4):
                    q, c = j // 2, j % 2
                    if j == 0:
                        dve.wait_ge(taps, base + 1)
                    dve.wait_ge(glu_s, 4 * i + j + 1)
                    nc.vector.scalar_tensor_tensor(
                        out=u[:, j, PAD:PAD + LEN], in0=ps[:, 4 * q + c, 0:LEN],
                        scalar=par_now[:, j * PAR:j * PAR + 1], in1=glu_sig[:, j, :],
                        op0=ALU.add, op1=ALU.mult).then_inc(taps, 1)
                    if c == 1:
                        count = 1 + 2 * (q + 1) + 2 * TAPS * q
                        for k in range(TAPS):
                            for jj in (j - 1, j):
                                tap = par_now[:, jj * PAR + 5 + k:jj * PAR + 6 + k]
                                src = u[:, jj, k:k + SEQ]
                                dst = acc[:, jj, :] if k < TAPS - 1 else \
                                    conv[:, ds(4 * i + jj, 1), :].rearrange("p o t -> p (o t)")
                                dve.wait_ge(taps, base + count - 1)
                                if k == 0:
                                    ins = nc.vector.tensor_scalar(dst, src, tap, par_now[:, jj * PAR + 2:jj * PAR + 3],
                                                                  ALU.mult, ALU.add)
                                else:
                                    ins = nc.vector.scalar_tensor_tensor(out=dst, in0=src, scalar=tap,
                                                                         in1=acc[:, jj, :], op0=ALU.mult,
                                                                         op1=ALU.add)
                                ins.then_inc(taps, 1)
                                count += 1

            conv_pass(0)
            with dve.Fori(1, 4) as i:
                conv_pass(i)

            dve.wait_ge(sums, 1)
            done(nc.vector.tensor_copy(mean_sb[:, :], ps[:, 0, 0:SEQ]))
            for c in range(4):
                part = conv[:, 4 * c:4 * c + 4, :]
                nc.vector.tensor_tensor(part, part, mean_sb[:, :].rearrange("p (o t) -> p o t", o=1)
                                        .broadcast_to([P, 4, SEQ]), ALU.subtract).then_inc(centred, 1)
            dve.wait_ge(sums, 2)
            nc.vector.tensor_scalar(rstd_c[:, :], ps[:, 1, 0:SEQ], LN_EPS, None, ALU.add).then_inc(var_in, 1)
            dve.wait_ge(root, 1)
            done(nc.vector.reciprocal(rstd_c[:, :], rstd_c[:, :]))
            for c in range(4):
                part = conv[:, 4 * c:4 * c + 4, :]
                nc.vector.tensor_tensor(part, part, rstd_c[:, :].rearrange("p (o t) -> p o t", o=1)
                                        .broadcast_to([P, 4, SEQ]), ALU.mult).then_inc(scaled, 1)

            def norm_stats(t, var_s):
                for c in range(4):
                    ins = nc.vector.bn_stats(stats[:, t, c, :], h[:, t, c * 512:(c + 1) * 512])
                done(ins)
                done(nc.vector.bn_aggr(mv[:, t, :], stats[:, t, :, :].rearrange("p c s -> p (c s)")))
                nc.vector.tensor_scalar(rstd[:, t:t + 1], mv[:, t, 1:2], LN_EPS, None, ALU.add).then_inc(var_s, 1)

            def norm_apply(t, root_s, ready):
                dve.wait_ge(root_s, t + 1)
                done(nc.vector.reciprocal(rstd[:, t:t + 1], rstd[:, t:t + 1]))
                done(nc.vector.scalar_tensor_tensor(out=h[:, t, :], in0=h[:, t, :], scalar=mv[:, t, 0:1],
                                                    in1=gain[:, :], op0=ALU.subtract, op1=ALU.mult))
                nc.vector.scalar_tensor_tensor(out=h[:, t, :], in0=h[:, t, :], scalar=rstd[:, t:t + 1],
                                               in1=bias[:, :], op0=ALU.mult, op1=ALU.add).then_inc(ready, 1)

            dve.wait_ge(x_s, 16)
            dve.wait_ge(gain_s, 16)
            dve.wait_ge(bias_s, 16)
            for t in range(TT):
                if t == 0:
                    dve.wait_ge(pw2, 1)
                else:
                    dve.wait_ge(freed[(KT - 1) % CONV_SLOTS], 4 + KT // CONV_SLOTS)
                done(nc.vector.scalar_tensor_tensor(
                    out=h[:, t, :], in0=h[:, t, :], scalar=ALPHA,
                    in1=ps[:, 4 * t:4 * t + 4, :].rearrange("p b n -> p (b n)"), op0=ALU.mult, op1=ALU.add))
                norm_stats(t, var1)
                norm_apply(t, root1, h_ready)
            for t in range(TT):
                dve.wait_ge(hT_ps, t + 1)
                nc.vector.tensor_copy(hT[:, 8:16, t * P:(t + 1) * P],
                                      ps[:, 4 * t + 2:4 * t + 4, :].rearrange("p b (k c) -> p (b k) c", c=P)
                                      ).then_inc(hT_sb, 1)

            dve.wait_ge(consts, N_CONSTS)
            dve.wait_ge(rb_s, 16)
            dve.wait_ge(scores_s, 1)
            rb_b = rb[:, :].rearrange("p (o e) -> p o e", o=1).broadcast_to([P, TT, E])
            done(nc.vector.tensor_tensor(sel[:, :, :], score[:, :, :], rb_b, ALU.add))
            for t in range(TT):
                for g in range(GROUPS):
                    ins = nc.vector.max(top8[:, t, g, :], sel[:, t, g * PER:(g + 1) * PER])
            done(ins)
            done(nc.vector.tensor_tensor(gscore[:, :, :], top8[:, :, :, 0], top8[:, :, :, 1], ALU.add))
            done(nc.vector.tensor_reduce(gbest[:, :], gscore[:, :, :], AX.X, ALU.max))
            gb = gbest[:, :].rearrange("p (t o) -> p t o", o=1).broadcast_to([P, TT, GROUPS])
            gr = grank[:, :].rearrange("p (o g) -> p o g", o=1).broadcast_to([P, TT, GROUPS])
            done(nc.vector.tensor_tensor(gmark[:, :, :], gscore[:, :, :], gb, ALU.is_equal))
            done(nc.vector.tensor_tensor(gmark[:, :, :], gmark[:, :, :], gr, ALU.mult))
            done(nc.vector.tensor_reduce(gfirst[:, :], gmark[:, :, :], AX.X, ALU.max))
            gf = gfirst[:, :].rearrange("p (t o) -> p t o", o=1).broadcast_to([P, TT, GROUPS])
            done(nc.vector.tensor_tensor(gmark[:, :, :], gr, gf, ALU.is_equal))
            done(nc.vector.tensor_scalar(gmark[:, :, :], gmark[:, :, :], -1.0, 1e30, ALU.add, ALU.mult))
            for t in range(TT):
                ins = nc.vector.tensor_tensor(
                    sel_in[:, t, :].rearrange("p (g e) -> p g e", g=GROUPS),
                    sel[:, t, :].rearrange("p (g e) -> p g e", g=GROUPS),
                    gmark[:, t, :].rearrange("p (g o) -> p g o", o=1).broadcast_to([P, GROUPS, PER]), ALU.add)
            done(ins)
            for t in range(TT):
                done(nc.vector.max(best[:, t, :], sel_in[:, t, :]))
                done(nc.vector.max_index(best_at[:, t, :], best[:, t, :], sel_in[:, t, :]))
            done(nc.vector.tensor_copy(best_f[:, :, :], best_at[:, :, 0:2]))
            no_b = expert_no[:, :].rearrange("p (o e) -> p o e", o=1).broadcast_to([P, TT, E])
            for k in range(2):
                ins = nc.vector.tensor_tensor(hot[:, k, :, :], no_b,
                                              best_f[:, :, k:k + 1].broadcast_to([P, TT, E]), ALU.is_equal)
            done(ins)
            nc.vector.tensor_tensor(routed[:, :, :], hot[:, 0, :, :], hot[:, 1, :, :], ALU.add
                                    ).then_inc(routed_s, 1)
            dve.wait_ge(routed_s, 1)
            t2 = token2[:, :].rearrange("p (t o) -> p t o", o=1).broadcast_to([P, TT, E])
            done(nc.vector.tensor_scalar(rows[:, :, :, 0], t2, -BIG, None, ALU.add))
            done(nc.vector.tensor_tensor(rows[:, :, :, 1], t2, hot[:, 1, :, :], ALU.add))
            done(nc.vector.tensor_scalar(rows[:, :, :, 1], rows[:, :, :, 1], 2.0, -BIG, ALU.mult, ALU.add))
            dve.wait_ge(ranks_ps, 1)
            ps_rank = ps[:, 1, 0:TT * E].rearrange("p (t e) -> p t e", t=TT)
            done(nc.vector.scalar_tensor_tensor(out=rank[:, :, :], in0=ps_rank, scalar=1.0,
                                                in1=routed[:, :, :], op0=ALU.add, op1=ALU.mult))
            done(nc.vector.tensor_scalar(rank[:, :, :], rank[:, :, :], -1.0, None, ALU.add))
            done(nc.vector.reduce_max(most[:, :], ps[:, 2, 0:E], AX.X))
            nc.vector.memset(more[:, 0:1], E / 2.0)
            for b in range(1, BLOCKS):
                ins = nc.vector.tensor_scalar(more[:, b:b + 1], most[:, :], float(b * SLOTS), E / 2.0,
                                              ALU.is_gt, ALU.mult)
            done(ins)
            done(nc.vector.reduce_sum(pairs_f[:, :], more[:, :], AX.X))
            nc.vector.tensor_copy(pairs_i[:, :], pairs_f[:, :]).then_inc(pairs_s, 1)

            def pick_slots(m, q):
                e, b = expert_of(m), block_of(m)
                wait(dve, idx_ps, m - 1)
                nc.vector.tensor_tensor(
                    pick[:, q, :, :],
                    slot_no[:, ds(b, 1), :, :].rearrange("p o g s -> p o (g s)").broadcast_to([P, TT, P]),
                    rank[:, :, ds(e, 1)].broadcast_to([P, TT, P]), ALU.is_equal).then_inc(picked_s, 1)

            def indices(m, q, scatters):
                dve.wait_ge(idx_ps, m + 1)
                wait(dve, scattered[q], 16 * scatters)
                nc.vector.tensor_tensor(g_at[q][:, :], ps_idx[:, 0:1], half_off[:, :], ALU.add)
                nc.vector.tensor_tensor(s_at[q][:, :], ps_idx[:, 1:2], half_off[:, :], ALU.add
                                        ).then_inc(idx_sb, 1)

            pick_slots(0, 0)
            for k in range(2):
                for t in range(TT):
                    nc.vector.tensor_tensor_reduce(out=picked[:, :], in0=score[:, t, :], in1=hot[:, k, t, :],
                                                   scale=1.0, scalar=0.0, op0=ALU.mult, op1=ALU.add,
                                                   accum_out=gates[:, k, t:t + 1]).then_inc(step, 1)
                    n_step[0] += 1
                    dve.wait_ge(step, n_step[0])
            done(nc.vector.tensor_tensor(gsum[:, :], gates[:, 0, :], gates[:, 1, :], ALU.add))
            done(nc.vector.reciprocal(gsum[:, :], gsum[:, :]))
            for k in range(2):
                ins = nc.vector.tensor_tensor(gates[:, k, :], gates[:, k, :], gsum[:, :], ALU.mult)
            done(ins)
            indices(0, 0, 0)
            more_pairs = load_pairs(dve)

            def pair(i):
                for q in range(2):
                    n = 2 * i + q
                    pick_slots(n + 1, 1 - q)
                    indices(n + 1, 1 - q, i + q)
                    dve.wait_ge(act_done, n + 1)
                    chunk_used(dve, UP_END, n + 1)
                    wait(dve, midT_ps, n)
                    nc.vector.tensor_tensor(mid, act_sb, ps_u, ALU.mult).then_inc(mid_done, 1)
                    dve.wait_ge(midT_ps, n + 1)
                    chunk_used(dve, DOWN_END, n)
                    nc.vector.tensor_copy(midT, ps_mid.rearrange("p (c s) -> p c s", c=2)
                                          ).then_inc(midT_sb, 1)
                    chunk_used(dve, DOWN_END, n + 1)
                    wait(dve, scattered[q], 16 * i)
                    nc.vector.tensor_copy(y[q][:, 512:1024], ps_y[:, 1, :]).then_inc(y_sb[1], 1)

            pair(0)
            dve.wait_ge(h_stored, 16 * TT)
            nc.vector.tensor_scalar(h[:, :, :], h[:, :, :], ALPHA, None, ALU.mult).then_inc(alpha_h, 1)
            with dve.Fori(1, E // 2) as i:
                pair(i)
            with dve.If(more_pairs > E // 2):
                with dve.Fori(E // 2, more_pairs) as i:
                    pair(i)

            dve.wait_ge(alpha_h, 1)
            dve.wait_ge(gain2_s, 16)
            dve.wait_ge(bias2_s, 16)
            for t in range(TT):
                dve.wait_ge(y_in[t], 16)
                for k in range(2):
                    done(nc.vector.scalar_tensor_tensor(
                        out=h[:, t, :], in0=ring[:, 2 * t + k, :], scalar=gates[:, k, t:t + 1], in1=h[:, t, :],
                        op0=ALU.mult, op1=ALU.add))
                norm_stats(t, var2)
                norm_apply(t, root2, out_ready)

        @block.tensor
        def _(pe):
            def pw1_pair(i, q):
                wait(pe, glu_s, 4 * (i - 1) + 2 * q + 2)
                wait(pe, taps, (i - 1) * TAP_OPS + 1 + 2 * (q + 1) + 2 * TAPS * q)
                for c in range(4):
                    s = 4 * q + c
                    pe.wait_ge(arrived[s], 16 * i + 16)
                    chunk = ring[:, s, :].rearrange("p (k n) -> p k n", k=8)
                    for ct in range(2):
                        bank = 4 * q + 2 * (c // 2) + ct
                        for k in range(8):
                            kk = 8 * (c % 2) + k
                            mm = nc.tensor.matmul(ps[:, bank, 0:LEN], chunk[:, k, ct * P:(ct + 1) * P],
                                                  xT[:, kk, :], start=(kk == 0), stop=(kk == KT - 1))
                    mm.then_inc(freed[s], 1)

            def pw1_pass(i):
                for q in range(2):
                    pw1_pair(i, q)

            pe.wait_ge(xT_in_s[0], 16)
            pe.wait_ge(xT_in_s[1], 16)
            pw1_pass(0)
            with pe.Fori(1, 4) as i:
                pw1_pass(i)

            pe.wait_ge(consts, N_CONSTS)
            pe.wait_ge(taps, 3 * TAP_OPS + 3)
            for k in range(KT):
                if k % 2 == 0:
                    pe.wait_ge(taps, (k // 4) * TAP_OPS + 1 + (2 + 2 * TAPS) * (k % 4 // 2 + 1))
                mm = nc.tensor.matmul(ps[:, 0, 0:SEQ], mean_w[:, :], conv[:, k, :], start=(k == 0), stop=(k == KT - 1))
            mm.then_inc(sums, 1)
            for k in range(KT):
                if k % 4 == 0:
                    pe.wait_ge(squared, k // 4 + 1)
                mm = nc.tensor.matmul(ps[:, 1, 0:SEQ], mean_w[:, :], squares[:, k, :], start=(k == 0),
                                      stop=(k == KT - 1))
            mm.then_inc(sums, 1)

            pe.wait_ge(b2_s, 16)
            pe.wait_ge(silu_c, 1)
            for t in range(TT):
                for nb in range(4):
                    nc.tensor.matmul(ps[:, 4 * t + nb, :], ones[0:1, :], b2_row[0:1, nb * 512:(nb + 1) * 512],
                                     start=True, stop=False)
            for k in range(KT):
                s = k % CONV_SLOTS
                pe.wait_ge(silu_c, k + 1)
                pe.wait_ge(arrived[s], 16 * (4 + k // CONV_SLOTS + 1))
                for t in range(TT):
                    for nb in range(4):
                        mm = nc.tensor.matmul(ps[:, 4 * t + nb, :], conv[:, k, t * P:(t + 1) * P],
                                              ring[:, s, nb * 512:(nb + 1) * 512],
                                              start=False, stop=(k == KT - 1))
                    if k == KT - 1 and t == 0:
                        mm.then_inc(pw2, 1)
                mm.then_inc(freed[s], 1)

            for t in range(TT):
                pe.wait_ge(h_ready, t + 1)
                for k in range(KT):
                    mm = nc.tensor.transpose(ps[:, 4 * t + k // 4, (k % 4) * P:(k % 4 + 1) * P],
                                             h[:, t, k * P:(k + 1) * P], ident[:, :])
                mm.then_inc(hT_ps, 1)
            pe.wait_ge(rw_s, 16)
            pe.wait_ge(hT_sb, 2 * TT)
            for t in range(TT):
                for k in range(KT):
                    mm = nc.tensor.matmul(ps[:, 0, t * E:(t + 1) * E], hT[:, k, t * P:(t + 1) * P],
                                          rw[:, k * E:(k + 1) * E], start=(k == 0), stop=(k == KT - 1))
            mm.then_inc(logits, 1)
            pe.wait_ge(routed_s, 1)
            nc.tensor.matmul(ps[:, 1, 0:E], before[:, :], routed[:, 0, :], start=True, stop=True)
            nc.tensor.matmul(ps[:, 1, E:2 * E], ones[:, :], routed[:, 0, :], start=True, stop=False)
            nc.tensor.matmul(ps[:, 1, E:2 * E], before[:, :], routed[:, 1, :], start=False, stop=True)
            nc.tensor.matmul(ps[:, 2, 0:E], ones[:, :], routed[:, 0, :], start=True, stop=False)
            nc.tensor.matmul(ps[:, 2, 0:E], ones[:, :], routed[:, 1, :], start=False, stop=True
                             ).then_inc(ranks_ps, 1)

            def slot_rows(m, q):
                pe.wait_ge(picked_s, m + 1)
                wait(pe, idx_sb, m)
                for t in range(TT):
                    mm = nc.tensor.matmul(ps_idx, pick[:, q, t, :],
                                          rows[:, t, ds(expert_of(m), 1), :].rearrange("p o r -> p (o r)"),
                                          start=(t == 0), stop=(t == TT - 1))
                mm.then_inc(idx_ps, 1)

            def transpose_rows(m, q, gathers):
                pe.wait_ge(gathered[q], 16 * gathers)
                wait(pe, xT_sb, m)
                for c in range(8):
                    mm = nc.tensor.transpose(ps_xT[:, c // 4, (c % 4) * P:(c % 4 + 1) * P],
                                             xg[q][:, c:1024:8], ident[:, :])
                mm.then_inc(xT_ps, 1)

            def chunk_landed(j, n):
                s = slot_of(j)
                pe.wait_ge(arrived[s], 16 * (used_before(s) + n) + 16)
                return s

            def pair(i):
                for q in range(2):
                    n = 2 * i + q
                    pe.wait_ge(xT_sb, n + 1)
                    wait(pe, act_done, n)
                    wait(pe, mid_done, n)
                    for j in range(8):
                        kind, g, c0 = CHUNKS[j]
                        s = chunk_landed(j, n)
                        chunk = ring[:, s, :].rearrange("p (c f) -> p c f", c=4)
                        dst = ps_g if kind == "gate" else ps_u
                        for c in range(4):
                            for hh in range(2):
                                mm = nc.tensor.matmul(dst[hh * SLOTS:(hh + 1) * SLOTS, :],
                                                      xgT[q][:, c0 + c, g * SLOTS:(g + 1) * SLOTS],
                                                      chunk[:, c, hh * 256:(hh + 1) * 256],
                                                      start=(g == 0 and c0 + c == 0),
                                                      stop=(g == 1 and c0 + c == 7))
                        mm.then_inc(freed[s], 1)
                        if j == 1:
                            slot_rows(n + 1, 1 - q)
                    transpose_rows(n + 1, 1 - q, i + q + 1)
                    pe.wait_ge(mid_done, n + 1)
                    wait(pe, midT_sb, n)
                    for c in range(2):
                        mm = nc.tensor.transpose(ps_mid[:, c * P:(c + 1) * P], mid[:, c * P:(c + 1) * P], ident[:, :])
                    mm.then_inc(midT_ps, 1)
                    pe.wait_ge(midT_sb, n + 1)
                    wait(pe, y_sb[0], n)
                    wait(pe, y_sb[1], n)
                    for f in range(4):
                        s = chunk_landed(8 + f, n)
                        for nb in range(2):
                            for g in range(2):
                                mm = nc.tensor.matmul(ps_y[g * SLOTS:(g + 1) * SLOTS, nb, :],
                                                      midT[:, f % 2, (f // 2) * SLOTS:(f // 2 + 1) * SLOTS],
                                                      ring[:, s, g * 1024 + nb * 512:g * 1024 + (nb + 1) * 512],
                                                      start=(f == 0), stop=(f == 3))
                        mm.then_inc(freed[s], 1)

            slot_rows(0, 0)
            transpose_rows(0, 0, 1)
            more_pairs = load_pairs(pe)
            item_loop(pe, pair, more_pairs)


def kernel(**inputs):
    import numpy as np
    import concourse.bacc as bacc
    from concourse import mybir as _mybir
    from concourse.bass_utils import run_bass_kernel_spmd

    inp = {n: np.asarray(a) for n, a in inputs.items()}
    tokens = np.concatenate([inp["meta_tokens"], inp["x"][0]], axis=0)
    tiles = [inp["conv_pw1_b"][0][:D].reshape(KT, P), inp["conv_pw1_b"][0][D:].reshape(KT, P),
             inp["conv_dw_b"][0].reshape(KT, P), inp["conv_ln_g"][0].reshape(KT, P), inp["conv_ln_b"][0].reshape(KT, P)]
    tiles += [tap.reshape(KT, P) for tap in inp["conv_dw_w"][0]]
    par = np.stack(tiles, axis=0).transpose(2, 1, 0).reshape(P, KT * PAR)
    rw = inp["router_w"].reshape(KT, P, E).transpose(1, 0, 2).reshape(P, KT * E)
    arrays = {
        "xT": tokens.T, "x": inp["x"][0], "par": par, "w1": inp["conv_pw1_w"][0], "w2": inp["conv_pw2_w"][0],
        "b2": inp["conv_pw2_b"], "ln1_g": inp["ln_mix_g"], "ln1_b": inp["ln_mix_b"],
        "ln2_g": inp["ln_ffn_g"], "ln2_b": inp["ln_ffn_b"], "rw": rw, "rb": inp["router_b"].reshape(1, E),
        "wg": inp["moe_w_gate"][0], "wu": inp["moe_w_up"][0], "wd": inp["moe_w_down"][0],
    }
    arrays = {f"in_{n}": np.ascontiguousarray(a) for n, a in arrays.items()}

    nc = bacc.Bacc("TRN2", target_bir_lowering=False, num_devices=1)
    args = [nc.dram_tensor(n, a.shape, _mybir.dt.from_np(a.dtype), kind="ExternalInput").ap()
            for n, a in arrays.items()]
    out = nc.dram_tensor("out", (SEQ, D), _mybir.dt.float32, kind="ExternalOutput").ap()
    build(nc, *args, out)
    result = run_bass_kernel_spmd(nc, [arrays], core_ids=[0])
    return result.results[0]["out"].reshape(1, SEQ, D)
```

```python
import concourse.bass as bass
from concourse import mybir
from concourse.bass import ds
from contextlib import ExitStack

D = 2048
SEQ = 256
META = 16
LEN = META + SEQ
TAPS = 31
E = 32
GROUPS = 4
PER = E // GROUPS
FF = 512
P = 128
KT = D // P
TT = SEQ // P
SLOTS = 64
BLOCKS = SEQ // SLOTS
ALPHA = 2.0 ** 0.25
LN_EPS = 1e-5
PAD = TAPS - 1 - META
PAR = 5 + TAPS
RING = 12
CONV_SLOTS = 8
LOOKUPS = BLOCKS + 1
N_CONSTS = 7
TAP_OPS = 1 + 4 + 4 * TAPS


def build(nc, xT_in, x_in, par_in, w1, w2, b2, ln1_g, ln1_b, ln2_g, ln2_b, rw_in, rb_in, wg, wu, wd, out):
    f32, u32, i32 = mybir.dt.float32, mybir.dt.uint32, mybir.dt.int32
    ALU, ACT, AX = mybir.AluOpType, mybir.ActivationFunctionType, mybir.AxisListType

    ctx = ExitStack()
    with ctx:
        def sb(name, shape, dt=f32):
            return ctx.enter_context(nc.sbuf_tensor(name, shape, dt))

        def sem(name):
            return ctx.enter_context(nc.semaphore(name))

        ring = sb("ring", [P, RING, 2048])
        xT = sb("xT", [P, KT, LEN])
        squares = xT[:, :, 0:SEQ]
        hT = xT[:, :, 0:SEQ]
        total = xT[:, :, 0:SEQ]
        conv = sb("conv", [P, KT, SEQ])
        h = sb("h", [P, TT, D])
        gain = sb("gain", [P, D])
        bias = sb("bias", [P, D])
        par = sb("par", [P, KT * PAR])
        par_now = sb("par_now", [P, 4 * PAR])
        glu_sig = sb("glu_sig", [P, 4, LEN])
        u = sb("u", [P, 4, PAD + LEN])
        acc = sb("acc", [P, 4, SEQ])
        mean_sb = sb("mean_sb", [P, SEQ])
        rstd_c = sb("rstd_c", [P, SEQ])
        var_c = sb("var_c", [P, SEQ])
        newton = sb("newton", [P, SEQ])
        b2_row = sb("b2_row", [1, D])
        ones = sb("ones", [P, P])
        mean_w = sb("mean_w", [P, P])
        ident = sb("ident", [P, P])
        before = sb("before", [P, P])
        rw = sb("rw", [P, KT * E])
        rb = sb("rb", [P, E])
        stats = sb("stats", [P, TT, 4, 6])
        mv = sb("mv", [P, TT, 2])
        rstd = sb("rstd", [P, TT])
        score = sb("score", [P, TT, E])
        sel = sb("sel", [P, TT, E])
        top8 = sb("top8", [P, TT, GROUPS, 8])
        gscore = sb("gscore", [P, TT, GROUPS])
        gbest = sb("gbest", [P, TT])
        gmark = sb("gmark", [P, TT, GROUPS])
        gfirst = sb("gfirst", [P, TT])
        grank = sb("grank", [P, GROUPS])
        sel_in = sb("sel_in", [P, TT, E])
        best = sb("best", [P, TT, 8])
        best_at = sb("best_at", [P, TT, 8], u32)
        best_f = sb("best_f", [P, TT, 2])
        hot = sb("hot", [P, 2, TT, E])
        gates = sb("gates", [P, 2, TT])
        gsum = sb("gsum", [P, TT])
        picked = sb("picked", [P, E])
        routed = sb("routed", [P, TT, E])
        rank = sb("rank", [P, TT, E])
        weight = sb("weight", [P, TT, E])
        expert_no = sb("expert_no", [P, E])
        most = sb("most", [P, 1])
        more = sb("more", [P, BLOCKS])
        pairs_f = sb("pairs_f", [P, 1])
        pairs_i = sb("pairs_i", [P, 1], i32)
        slot_no = sb("slot_no", [P, LOOKUPS, SLOTS])
        pick = sb("pick", [P, TT, 2, SLOTS])
        pick_w = sb("pick_w", [P, TT, 2, SLOTS])
        pickT = sb("pickT", [P, TT, P])
        y = conv[:, 0:8, :].rearrange("p k c -> p (k c)")
        xgT = conv[:, 8:16, :].rearrange("p k (a i s) -> p (k a) i s", a=2, i=2)
        act_sb, mid = acc[:, 0, :], acc[:, 1, :]
        midT = acc[:, 2, :].rearrange("p (c s) -> p c s", c=2)

        ps = ctx.enter_context(nc.psum_tensor("ps", [P, 8, 512], f32))
        ps_gu, ps_mid, ps_pT = ps[:, 0, :], ps[:, 1, 0:256], ps[:, 1, 256:512]
        ps_y, ps_x, ps_add = ps[:, 2:4, :], ps[:, 4:6, :], ps[:, 6:8, :]

        arrived = [sem(f"arrived{s}") for s in range(RING)]
        freed = [sem(f"freed{s}") for s in range(RING)]
        xT_in_s = [sem("xT_lo"), sem("xT_hi")]
        par_s, x_s, b2_s, gain_s, bias_s, rw_s, rb_s = (
            sem(n) for n in ("par_in", "x_in", "b2_in", "gain_in", "bias_in", "rw_in", "rb_in"))
        consts = sem("consts")
        marks = sem("marks")
        glu_s = sem("glu_s")
        taps = sem("taps")
        sums = sem("sums")
        centred = sem("centred")
        squared = sem("squared")
        var_in = sem("var_in")
        root = sem("root")
        scaled = sem("scaled")
        silu_c = sem("silu_c")
        pw2 = sem("pw2")
        step = sem("step")
        root1 = sem("root1")
        var1 = sem("var1")
        h_ready = sem("h_ready")
        hT_ps = sem("hT_ps")
        hT_sb = sem("hT_sb")
        logits = sem("logits")
        scores_s = sem("scores")
        routed_s = sem("routed_s")
        ranks_ps = sem("ranks_ps")
        pairs_s = sem("pairs_s")
        picked_s = sem("picked_s")
        weighted = sem("weighted")
        pT_ps = sem("pT_ps")
        pT_sb = sem("pT_sb")
        x_ps = sem("x_ps")
        x_sb = sem("x_sb")
        add_ps = sem("add_ps")
        added = sem("added")
        act_done = sem("act_done")
        mid_done = sem("mid_done")
        midT_ps = sem("midT_ps")
        midT_sb = sem("midT_sb")
        y_sb = [sem("y_sb_act"), sem("y_sb_dve")]
        all_added = sem("all_added")
        total_0 = sem("total_0")
        gain2_s, bias2_s = sem("gain2_in"), sem("bias2_in")
        var2, root2 = sem("var2"), sem("root2")
        out_ready = sem("out_ready")
        out_s = sem("out_s")

        block = ctx.enter_context(nc.Block())

        def wait(eng, s, value):
            if isinstance(value, int) and value <= 0:
                return
            eng.wait_ge(s, value)

        w1_v = w1.rearrange("(k p) n -> p k n", p=P)
        wg_v = wg.rearrange("e (g p c) n -> e g p (c n)", g=2, c=8)
        wu_v = wu.rearrange("e (g p c) n -> e g p (c n)", g=2, c=8)
        wd_v = wd.rearrange("e (f p) n -> e f p n", p=P)

        CHUNKS = []
        for g in range(2):
            for c0 in (0, 4):
                CHUNKS += [("gate", g, c0), ("up", g, c0)]
        CHUNKS += [("down", f, 0) for f in range(4)]

        def slot_of(j):
            return (CONV_SLOTS + j) % RING

        def used_before(s):
            return 8 * 4 // CONV_SLOTS + KT // CONV_SLOTS if s < CONV_SLOTS else 0

        def chunk_used(eng, j, items):
            if not (isinstance(items, int) and items <= 0):
                eng.wait_ge(freed[slot_of(j)], used_before(slot_of(j)) + items)

        def signal_of(j):
            return slot_of(j + 1 if CHUNKS[j][0] == "gate" else j)

        def n_is_first(n):
            return isinstance(n, int) and n == 0

        UP_END, DOWN_END = 7, 11

        def expert_of(m):
            return m % E

        def block_of(m):
            return m // E

        def item_loop(eng, body, more_pairs):
            body(0)
            with eng.Fori(1, E // 2) as i:
                body(i)
            with eng.If(more_pairs > E // 2):
                with eng.Fori(E // 2, more_pairs) as i:
                    body(i)

        def load_pairs(eng):
            eng.wait_ge(pairs_s, 1)
            return eng.value_load(pairs_i[0:1, 0:1], min_val=E // 2, max_val=BLOCKS * E // 2)

        @block.sync
        def _(sp):
            def pw1_chunks(i):
                for q in range(2):
                    for c in range(4):
                        s = 4 * q + c
                        col = (c // 2) * D + (2 * i + q) * 256
                        wait(sp, freed[s], i)
                        k0 = 8 * (c % 2)
                        sp.dma_start(ring[:, s, :].rearrange("p (k n) -> p k n", k=8),
                                     w1_v[:, k0:k0 + 8, ds(col, 256)]).then_inc(arrived[s], 16)

            sp.dma_start(par[:, :], par_in).then_inc(par_s, 16)
            for half in range(2):
                sp.dma_start(xT[:, 8 * half:8 * half + 8, :],
                             xT_in.rearrange("(k p) t -> p k t", p=P)[:, 8 * half:8 * half + 8, :]
                             ).then_inc(xT_in_s[half], 16)
            pw1_chunks(0)
            sp.dma_start(h[:, :, :], x_in.rearrange("(t p) d -> p t d", p=P)).then_inc(x_s, 16)
            sp.dma_start(b2_row[:, :], b2).then_inc(b2_s, 16)
            sp.dma_start(gain[:, :], ln1_g.broadcast_to([P, D])).then_inc(gain_s, 16)
            sp.dma_start(bias[:, :], ln1_b.broadcast_to([P, D])).then_inc(bias_s, 16)
            sp.dma_start(rw[:, :], rw_in).then_inc(rw_s, 16)
            sp.dma_start(rb[:, :], rb_in.broadcast_to([P, E])).then_inc(rb_s, 16)
            with sp.Fori(1, 4) as i:
                pw1_chunks(i)
            for k in range(KT):
                s = k % CONV_SLOTS
                sp.wait_ge(freed[s], 4 + k // CONV_SLOTS)
                sp.dma_start(ring[:, s, :], w2[k * P:(k + 1) * P, :]).then_inc(arrived[s], 16)

            def expert_chunks(n):
                e = expert_of(n)
                for j, (kind, a, c0) in enumerate(CHUNKS):
                    s = slot_of(j)
                    if n_is_first(n) and s >= CONV_SLOTS:
                        pass
                    elif s < CONV_SLOTS and n_is_first(n):
                        sp.wait_ge(freed[s], used_before(s))
                    else:
                        r = signal_of(j)
                        sp.wait_ge(freed[r], used_before(r) + n)
                    if kind == "down":
                        src = wd_v[ds(e, 1), a, :, :].rearrange("o p n -> (o p) n")
                    else:
                        src = (wg_v if kind == "gate" else wu_v)[ds(e, 1), a, :, c0 * FF:(c0 + 4) * FF]\
                            .rearrange("o p n -> (o p) n")
                    sp.dma_start(ring[:, s, :], src).then_inc(arrived[s], 16)

            def pair(i):
                for q in range(2):
                    expert_chunks(2 * i + q)

            pair(0)
            sp.wait_ge(h_ready, TT)
            sp.dma_start(gain[:, :], ln2_g.broadcast_to([P, D])).then_inc(gain2_s, 16)
            sp.dma_start(bias[:, :], ln2_b.broadcast_to([P, D])).then_inc(bias2_s, 16)
            more_pairs = load_pairs(sp)
            with sp.Fori(1, E // 2) as i:
                pair(i)
            with sp.If(more_pairs > E // 2):
                with sp.Fori(E // 2, more_pairs) as i:
                    pair(i)

            for t in range(TT):
                sp.wait_ge(out_ready, t + 1)
                sp.dma_start(out[t * P:(t + 1) * P, :], h[:, t, :]).then_inc(out_s, 16)
            sp.wait_ge(out_s, 16 * TT)

        @block.gpsimd
        def _(pool):
            n_marks = [0]

            def mark(ins):
                n_marks[0] += 1
                ins.then_inc(marks, 1)
                pool.wait_ge(marks, n_marks[0])

            def const(ins):
                ins.then_inc(consts, 1)

            const(nc.gpsimd.memset(ones[:, :], 1.0))
            const(nc.gpsimd.memset(mean_w[:, :], 1.0 / D))
            mark(nc.gpsimd.memset(ident[:, :], 0.0))
            const(nc.gpsimd.affine_select(out=ident[:, :], in_=ident[:, :], compare_op=ALU.not_equal, fill=1.0,
                                         base=0, pattern=[[-1, P]], channel_multiplier=1))
            mark(nc.gpsimd.memset(before[:, :], 0.0))
            const(nc.gpsimd.affine_select(out=before[:, :], in_=before[:, :], compare_op=ALU.is_ge, fill=1.0,
                                         base=0, pattern=[[-1, P]], channel_multiplier=1))
            fl = dict(allow_small_or_imprecise_dtypes=True)
            const(nc.gpsimd.iota(expert_no[:, :], [[1, E]], base=0, channel_multiplier=0, **fl))
            const(nc.gpsimd.iota(grank[:, :], [[-1, GROUPS]], base=GROUPS, channel_multiplier=0, **fl))
            const(nc.gpsimd.iota(slot_no[:, :, :], [[SLOTS, LOOKUPS], [1, SLOTS]], base=0,
                                 channel_multiplier=0, **fl))
        @block.scalar
        def _(act):
            act.wait_ge(par_s, 16)

            def gates_of(i):
                for j in range(4):
                    q, c = j // 2, j % 2
                    act.wait_ge(freed[4 * q + 3], i + 1)
                    wait(act, taps, (i - 1) * TAP_OPS + 5)
                    nc.scalar.activation(glu_sig[:, j, :], ps[:, 4 * q + 2 + c, 0:LEN], ACT.Sigmoid,
                                         bias=par[:, ds((4 * i + j) * PAR + 1, 1)]).then_inc(glu_s, 1)

            gates_of(0)
            with act.Fori(1, 4) as i:
                gates_of(i)

            for c in range(4):
                act.wait_ge(centred, c + 1)
                nc.scalar.activation(squares[:, 4 * c:4 * c + 4, :], conv[:, 4 * c:4 * c + 4, :], ACT.Square
                                     ).then_inc(squared, 1)
            act.wait_ge(var_in, 1)
            nc.scalar.activation(rstd_c[:, :], var_c[:, :], ACT.Sqrt).then_inc(root, 1)
            for k in range(KT):
                act.wait_ge(scaled, k // 4 + 1)
                nc.scalar.activation(conv[:, k, :], conv[:, k, :], ACT.Silu,
                                     scale=par[:, k * PAR + 3:k * PAR + 4],
                                     bias=par[:, k * PAR + 4:k * PAR + 5]).then_inc(silu_c, 1)
            for t in range(TT):
                act.wait_ge(var1, t + 1)
                nc.scalar.activation(rstd[:, t:t + 1], mv[:, t, 1:2], ACT.Sqrt).then_inc(root1, 1)
            for t in range(TT):
                act.wait_ge(hT_ps, t + 1)
                nc.scalar.activation(hT[:, 0:8, t * P:(t + 1) * P],
                                     ps[:, 4 * t:4 * t + 2, :].rearrange("p b (k c) -> p (b k) c", c=P),
                                     ACT.Copy).then_inc(hT_sb, 1)
            act.wait_ge(logits, 1)
            nc.scalar.activation(score[:, :, :], ps[:, 0, 0:TT * E].rearrange("p (t e) -> p t e", t=TT),
                                 ACT.Sigmoid).then_inc(scores_s, 1)
            more_pairs = load_pairs(act)

            def copy_x(p, g):
                act.wait_ge(x_ps, 2 * p + g + 1)
                chunk_used(act, UP_END, 2 * p)
                nc.scalar.activation(xgT[:, 8 * g:8 * g + 8, :, :], ps_x.rearrange(
                    "p b (k i s) -> p (b k) i s", i=2, s=SLOTS), ACT.Copy).then_inc(x_sb, 1)

            def pair(i):
                for q in range(2):
                    n = 2 * i + q
                    chunk_used(act, UP_END, n + 1)
                    wait(act, mid_done, n)
                    nc.scalar.activation(act_sb, ps_gu[:, 0:256], ACT.Silu).then_inc(act_done, 1)
                    if q == 1:
                        copy_x(i + 1, 0)
                    chunk_used(act, DOWN_END, n + 1)
                    wait(act, add_ps, 8 * i)
                    nc.scalar.activation(y[q * SLOTS:(q + 1) * SLOTS, 0:1024],
                                         ps_y[0:SLOTS, :, :].rearrange("p b n -> p (b n)"), ACT.Copy
                                         ).then_inc(y_sb[0], 1)
                copy_x(i + 1, 1)

            for g in range(2):
                copy_x(0, g)
            pair(0)
            with act.Fori(1, E // 2) as i:
                pair(i)
            with act.If(more_pairs > E // 2):
                with act.Fori(E // 2, more_pairs) as i:
                    pair(i)

            for t in range(TT):
                act.wait_ge(var2, t + 1)
                nc.scalar.activation(rstd[:, t:t + 1], mv[:, t, 1:2], ACT.Sqrt).then_inc(root2, 1)

        @block.vector
        def _(dve):
            n_step = [0]

            def done(ins):
                n_step[0] += 1
                ins.then_inc(step, 1)
                dve.wait_ge(step, n_step[0])

            def refine(root, var, tmp):
                done(nc.vector.tensor_tensor(tmp, root, root, ALU.mult))
                done(nc.vector.tensor_tensor(tmp, tmp, var, ALU.mult))
                done(nc.vector.tensor_scalar(tmp, tmp, -0.5, 1.5, ALU.mult, ALU.add))
                done(nc.vector.tensor_tensor(root, root, tmp, ALU.mult))

            done(nc.vector.memset(u[:, :, 0:PAD], 0.0))
            dve.wait_ge(par_s, 16)

            def conv_pass(i):
                base = i * TAP_OPS
                wait(dve, taps, base)
                nc.vector.tensor_copy(par_now[:, :], par[:, ds(4 * i * PAR, 4 * PAR)]).then_inc(taps, 1)
                for j in range(4):
                    q, c = j // 2, j % 2
                    if j == 0:
                        dve.wait_ge(taps, base + 1)
                    dve.wait_ge(glu_s, 4 * i + j + 1)
                    nc.vector.scalar_tensor_tensor(
                        out=u[:, j, PAD:PAD + LEN], in0=ps[:, 4 * q + c, 0:LEN],
                        scalar=par_now[:, j * PAR:j * PAR + 1], in1=glu_sig[:, j, :],
                        op0=ALU.add, op1=ALU.mult).then_inc(taps, 1)
                    if c == 1:
                        count = 1 + 2 * (q + 1) + 2 * TAPS * q
                        for k in range(TAPS):
                            for jj in (j - 1, j):
                                tap = par_now[:, jj * PAR + 5 + k:jj * PAR + 6 + k]
                                src = u[:, jj, k:k + SEQ]
                                dst = acc[:, jj, :] if k < TAPS - 1 else \
                                    conv[:, ds(4 * i + jj, 1), :].rearrange("p o t -> p (o t)")
                                dve.wait_ge(taps, base + count - 1)
                                if k == 0:
                                    ins = nc.vector.tensor_scalar(dst, src, tap, par_now[:, jj * PAR + 2:jj * PAR + 3],
                                                                  ALU.mult, ALU.add)
                                else:
                                    ins = nc.vector.scalar_tensor_tensor(out=dst, in0=src, scalar=tap,
                                                                         in1=acc[:, jj, :], op0=ALU.mult,
                                                                         op1=ALU.add)
                                ins.then_inc(taps, 1)
                                count += 1

            conv_pass(0)
            with dve.Fori(1, 4) as i:
                conv_pass(i)

            dve.wait_ge(sums, 1)
            done(nc.vector.tensor_copy(mean_sb[:, :], ps[:, 0, 0:SEQ]))
            for c in range(4):
                part = conv[:, 4 * c:4 * c + 4, :]
                nc.vector.tensor_tensor(part, part, mean_sb[:, :].rearrange("p (o t) -> p o t", o=1)
                                        .broadcast_to([P, 4, SEQ]), ALU.subtract).then_inc(centred, 1)
            dve.wait_ge(sums, 2)
            nc.vector.tensor_scalar(var_c[:, :], ps[:, 1, 0:SEQ], LN_EPS, None, ALU.add).then_inc(var_in, 1)
            dve.wait_ge(root, 1)
            done(nc.vector.reciprocal(rstd_c[:, :], rstd_c[:, :]))
            refine(rstd_c[:, :], var_c[:, :], newton[:, :])
            for c in range(4):
                part = conv[:, 4 * c:4 * c + 4, :]
                nc.vector.tensor_tensor(part, part, rstd_c[:, :].rearrange("p (o t) -> p o t", o=1)
                                        .broadcast_to([P, 4, SEQ]), ALU.mult).then_inc(scaled, 1)

            def norm_stats(t, var_s, src):
                for c in range(4):
                    ins = nc.vector.bn_stats(stats[:, t, c, :], src[:, c])
                done(ins)
                done(nc.vector.bn_aggr(mv[:, t, :], stats[:, t, :, :].rearrange("p c s -> p (c s)")))
                nc.vector.tensor_scalar(mv[:, t, 1:2], mv[:, t, 1:2], LN_EPS, None, ALU.add).then_inc(var_s, 1)

            def norm_apply(t, root_s, ready, src):
                def cols(a):
                    return a if len(src.shape) == 2 else a.rearrange("p (j c) -> p j c", c=src.shape[2])
                dve.wait_ge(root_s, t + 1)
                done(nc.vector.reciprocal(rstd[:, t:t + 1], rstd[:, t:t + 1]))
                refine(rstd[:, t:t + 1], mv[:, t, 1:2], newton[:, 0:1])
                done(nc.vector.scalar_tensor_tensor(out=cols(h[:, t, :]), in0=src, scalar=mv[:, t, 0:1],
                                                    in1=cols(gain[:, :]), op0=ALU.subtract, op1=ALU.mult))
                nc.vector.scalar_tensor_tensor(out=h[:, t, :], in0=h[:, t, :], scalar=rstd[:, t:t + 1],
                                               in1=bias[:, :], op0=ALU.mult, op1=ALU.add).then_inc(ready, 1)

            dve.wait_ge(x_s, 16)
            dve.wait_ge(gain_s, 16)
            dve.wait_ge(bias_s, 16)
            for t in range(TT):
                if t == 0:
                    dve.wait_ge(pw2, 1)
                else:
                    dve.wait_ge(freed[(KT - 1) % CONV_SLOTS], 4 + KT // CONV_SLOTS)
                done(nc.vector.scalar_tensor_tensor(
                    out=h[:, t, :], in0=h[:, t, :], scalar=ALPHA,
                    in1=ps[:, 4 * t:4 * t + 4, :].rearrange("p b n -> p (b n)"), op0=ALU.mult, op1=ALU.add))
                norm_stats(t, var1, h[:, t, :].rearrange("p (c n) -> p c n", c=4))
                norm_apply(t, root1, h_ready, h[:, t, :])
            for t in range(TT):
                dve.wait_ge(hT_ps, t + 1)
                nc.vector.tensor_copy(hT[:, 8:16, t * P:(t + 1) * P],
                                      ps[:, 4 * t + 2:4 * t + 4, :].rearrange("p b (k c) -> p (b k) c", c=P)
                                      ).then_inc(hT_sb, 1)

            dve.wait_ge(consts, N_CONSTS)
            dve.wait_ge(rb_s, 16)
            dve.wait_ge(scores_s, 1)
            rb_b = rb[:, :].rearrange("p (o e) -> p o e", o=1).broadcast_to([P, TT, E])
            done(nc.vector.tensor_tensor(sel[:, :, :], score[:, :, :], rb_b, ALU.add))
            for t in range(TT):
                for g in range(GROUPS):
                    ins = nc.vector.max(top8[:, t, g, :], sel[:, t, g * PER:(g + 1) * PER])
            done(ins)
            done(nc.vector.tensor_tensor(gscore[:, :, :], top8[:, :, :, 0], top8[:, :, :, 1], ALU.add))
            done(nc.vector.tensor_reduce(gbest[:, :], gscore[:, :, :], AX.X, ALU.max))
            gb = gbest[:, :].rearrange("p (t o) -> p t o", o=1).broadcast_to([P, TT, GROUPS])
            gr = grank[:, :].rearrange("p (o g) -> p o g", o=1).broadcast_to([P, TT, GROUPS])
            done(nc.vector.tensor_tensor(gmark[:, :, :], gscore[:, :, :], gb, ALU.is_equal))
            done(nc.vector.tensor_tensor(gmark[:, :, :], gmark[:, :, :], gr, ALU.mult))
            done(nc.vector.tensor_reduce(gfirst[:, :], gmark[:, :, :], AX.X, ALU.max))
            gf = gfirst[:, :].rearrange("p (t o) -> p t o", o=1).broadcast_to([P, TT, GROUPS])
            done(nc.vector.tensor_tensor(gmark[:, :, :], gr, gf, ALU.is_equal))
            done(nc.vector.tensor_scalar(gmark[:, :, :], gmark[:, :, :], -1.0, 1e30, ALU.add, ALU.mult))
            for t in range(TT):
                ins = nc.vector.tensor_tensor(
                    sel_in[:, t, :].rearrange("p (g e) -> p g e", g=GROUPS),
                    sel[:, t, :].rearrange("p (g e) -> p g e", g=GROUPS),
                    gmark[:, t, :].rearrange("p (g o) -> p g o", o=1).broadcast_to([P, GROUPS, PER]), ALU.add)
            done(ins)
            for t in range(TT):
                done(nc.vector.max(best[:, t, :], sel_in[:, t, :]))
                done(nc.vector.max_index(best_at[:, t, :], best[:, t, :], sel_in[:, t, :]))
            done(nc.vector.tensor_copy(best_f[:, :, :], best_at[:, :, 0:2]))
            no_b = expert_no[:, :].rearrange("p (o e) -> p o e", o=1).broadcast_to([P, TT, E])
            for k in range(2):
                ins = nc.vector.tensor_tensor(hot[:, k, :, :], no_b,
                                              best_f[:, :, k:k + 1].broadcast_to([P, TT, E]), ALU.is_equal)
            done(ins)
            nc.vector.tensor_tensor(routed[:, :, :], hot[:, 0, :, :], hot[:, 1, :, :], ALU.add
                                    ).then_inc(routed_s, 1)
            dve.wait_ge(routed_s, 1)
            dve.wait_ge(ranks_ps, 1)
            ps_rank = ps[:, 1, 0:TT * E].rearrange("p (t e) -> p t e", t=TT)
            done(nc.vector.scalar_tensor_tensor(out=rank[:, :, :], in0=ps_rank, scalar=1.0,
                                                in1=routed[:, :, :], op0=ALU.add, op1=ALU.mult))
            done(nc.vector.tensor_scalar(rank[:, :, :], rank[:, :, :], -1.0, None, ALU.add))
            done(nc.vector.reduce_max(most[:, :], ps[:, 2, 0:E], AX.X))
            nc.vector.memset(more[:, 0:1], E / 2.0)
            for b in range(1, BLOCKS):
                ins = nc.vector.tensor_scalar(more[:, b:b + 1], most[:, :], float(b * SLOTS), E / 2.0,
                                              ALU.is_gt, ALU.mult)
            done(ins)
            done(nc.vector.reduce_sum(pairs_f[:, :], more[:, :], AX.X))
            nc.vector.tensor_copy(pairs_i[:, :], pairs_f[:, :]).then_inc(pairs_s, 1)

            def pick_slots(p):
                wait(dve, x_ps, 2 * p)
                wait(dve, weighted, p)
                nc.vector.tensor_tensor(
                    pick[:, :, :, :],
                    slot_no[:, ds(block_of(2 * p), 1), :].rearrange("p (o i) s -> p o i s", o=1)
                    .broadcast_to([P, TT, 2, SLOTS]),
                    rank[:, :, ds(expert_of(2 * p), 2)].rearrange("p t (i o) -> p t i o", o=1)
                    .broadcast_to([P, TT, 2, SLOTS]), ALU.is_equal).then_inc(picked_s, 1)

            pick_slots(0)
            for k in range(2):
                for t in range(TT):
                    nc.vector.tensor_tensor_reduce(out=picked[:, :], in0=score[:, t, :], in1=hot[:, k, t, :],
                                                   scale=1.0, scalar=0.0, op0=ALU.mult, op1=ALU.add,
                                                   accum_out=gates[:, k, t:t + 1]).then_inc(step, 1)
                    n_step[0] += 1
                    dve.wait_ge(step, n_step[0])
            done(nc.vector.tensor_tensor(gsum[:, :], gates[:, 0, :], gates[:, 1, :], ALU.add))
            done(nc.vector.reciprocal(gsum[:, :], gsum[:, :]))
            for k in range(2):
                ins = nc.vector.tensor_tensor(gates[:, k, :], gates[:, k, :], gsum[:, :], ALU.mult)
            done(ins)
            for t in range(TT):
                done(nc.vector.tensor_scalar(weight[:, t, :], hot[:, 0, t, :], gates[:, 0, t:t + 1], None, ALU.mult))
                done(nc.vector.scalar_tensor_tensor(out=weight[:, t, :], in0=hot[:, 1, t, :],
                                                    scalar=gates[:, 1, t:t + 1], in1=weight[:, t, :],
                                                    op0=ALU.mult, op1=ALU.add))
            more_pairs = load_pairs(dve)

            def pair(i):
                dve.wait_ge(picked_s, i + 1)
                wait(dve, pT_ps, i)
                nc.vector.tensor_tensor(
                    pick_w[:, :, :, :], pick[:, :, :, :],
                    weight[:, :, ds(expert_of(2 * i), 2)].rearrange("p t (i o) -> p t i o", o=1)
                    .broadcast_to([P, TT, 2, SLOTS]), ALU.mult).then_inc(weighted, 1)
                pick_slots(i + 1)
                if isinstance(i, int):
                    nc.vector.tensor_scalar(total.rearrange("p (t j) c -> p t j c", t=TT),
                                            h[:, :, :].rearrange("p t (j c) -> p t j c", c=SEQ),
                                            ALPHA, None, ALU.mult).then_inc(total_0, 1)
                for q in range(2):
                    n = 2 * i + q
                    dve.wait_ge(act_done, n + 1)
                    wait(dve, midT_ps, n)
                    nc.vector.tensor_tensor(mid, act_sb, ps_gu[:, 256:512], ALU.mult).then_inc(mid_done, 1)
                    dve.wait_ge(midT_ps, n + 1)
                    chunk_used(dve, DOWN_END, n)
                    nc.vector.tensor_copy(midT, ps_mid.rearrange("p (c s) -> p c s", c=2)).then_inc(midT_sb, 1)
                    if q == 0:
                        dve.wait_ge(pT_ps, i + 1)
                        wait(dve, add_ps, 8 * i)
                        nc.vector.tensor_copy(pickT[:, :, :], ps_pT.rearrange("p (t c) -> p t c", t=TT)
                                              ).then_inc(pT_sb, 1)
                    chunk_used(dve, DOWN_END, n + 1)
                    wait(dve, add_ps, 8 * i)
                    nc.vector.tensor_copy(y[q * SLOTS:(q + 1) * SLOTS, 1024:2048],
                                          ps_y[SLOTS:P, :, :].rearrange("p b n -> p (b n)")).then_inc(y_sb[1], 1)
                if isinstance(i, int):
                    dve.wait_ge(total_0, 1)
                for t in range(TT):
                    for cb in range(4):
                        k = 4 * t + cb
                        dve.wait_ge(add_ps, 8 * i + k + 1)
                        part = total[:, 2 * k:2 * k + 2, :]
                        nc.vector.tensor_tensor(part, part,
                                                ps_add[:, k % 2, :].rearrange("p (j c) -> p j c", j=2),
                                                ALU.add).then_inc(added, 1)

            pair(0)
            with dve.Fori(1, E // 2) as i:
                pair(i)
            with dve.If(more_pairs > E // 2):
                with dve.Fori(E // 2, more_pairs) as i:
                    pair(i)
            dve.drain().then_inc(all_added, 1)
            dve.wait_ge(all_added, 1)

            dve.wait_ge(gain2_s, 16)
            dve.wait_ge(bias2_s, 16)
            for t in range(TT):
                src = total[:, 8 * t:8 * t + 8, :]
                norm_stats(t, var2, src.rearrange("p (c a) n -> p c a n", c=4))
                norm_apply(t, root2, out_ready, src)

        @block.tensor
        def _(pe):
            def pw1_pair(i, q):
                wait(pe, glu_s, 4 * (i - 1) + 2 * q + 2)
                wait(pe, taps, (i - 1) * TAP_OPS + 1 + 2 * (q + 1) + 2 * TAPS * q)
                for c in range(4):
                    s = 4 * q + c
                    pe.wait_ge(arrived[s], 16 * i + 16)
                    chunk = ring[:, s, :].rearrange("p (k n) -> p k n", k=8)
                    for ct in range(2):
                        bank = 4 * q + 2 * (c // 2) + ct
                        for k in range(8):
                            kk = 8 * (c % 2) + k
                            mm = nc.tensor.matmul(ps[:, bank, 0:LEN], chunk[:, k, ct * P:(ct + 1) * P],
                                                  xT[:, kk, :], start=(kk == 0), stop=(kk == KT - 1))
                    mm.then_inc(freed[s], 1)

            def pw1_pass(i):
                for q in range(2):
                    pw1_pair(i, q)

            pe.wait_ge(xT_in_s[0], 16)
            pe.wait_ge(xT_in_s[1], 16)
            pw1_pass(0)
            with pe.Fori(1, 4) as i:
                pw1_pass(i)

            pe.wait_ge(consts, N_CONSTS)
            pe.wait_ge(taps, 3 * TAP_OPS + 3)
            for k in range(KT):
                if k % 2 == 0:
                    pe.wait_ge(taps, (k // 4) * TAP_OPS + 1 + (2 + 2 * TAPS) * (k % 4 // 2 + 1))
                mm = nc.tensor.matmul(ps[:, 0, 0:SEQ], mean_w[:, :], conv[:, k, :], start=(k == 0), stop=(k == KT - 1))
            mm.then_inc(sums, 1)
            for k in range(KT):
                if k % 4 == 0:
                    pe.wait_ge(squared, k // 4 + 1)
                mm = nc.tensor.matmul(ps[:, 1, 0:SEQ], mean_w[:, :], squares[:, k, :], start=(k == 0),
                                      stop=(k == KT - 1))
            mm.then_inc(sums, 1)

            pe.wait_ge(b2_s, 16)
            pe.wait_ge(silu_c, 1)
            for t in range(TT):
                for nb in range(4):
                    nc.tensor.matmul(ps[:, 4 * t + nb, :], ones[0:1, :], b2_row[0:1, nb * 512:(nb + 1) * 512],
                                     start=True, stop=False)
            for k in range(KT):
                s = k % CONV_SLOTS
                pe.wait_ge(silu_c, k + 1)
                pe.wait_ge(arrived[s], 16 * (4 + k // CONV_SLOTS + 1))
                for t in range(TT):
                    for nb in range(4):
                        mm = nc.tensor.matmul(ps[:, 4 * t + nb, :], conv[:, k, t * P:(t + 1) * P],
                                              ring[:, s, nb * 512:(nb + 1) * 512],
                                              start=False, stop=(k == KT - 1))
                    if k == KT - 1 and t == 0:
                        mm.then_inc(pw2, 1)
                mm.then_inc(freed[s], 1)

            for t in range(TT):
                pe.wait_ge(h_ready, t + 1)
                for k in range(KT):
                    mm = nc.tensor.transpose(ps[:, 4 * t + k // 4, (k % 4) * P:(k % 4 + 1) * P],
                                             h[:, t, k * P:(k + 1) * P], ident[:, :])
                mm.then_inc(hT_ps, 1)
            pe.wait_ge(rw_s, 16)
            pe.wait_ge(hT_sb, 2 * TT)
            for t in range(TT):
                for k in range(KT):
                    mm = nc.tensor.matmul(ps[:, 0, t * E:(t + 1) * E], hT[:, k, t * P:(t + 1) * P],
                                          rw[:, k * E:(k + 1) * E], start=(k == 0), stop=(k == KT - 1))
            mm.then_inc(logits, 1)
            pe.wait_ge(routed_s, 1)
            nc.tensor.matmul(ps[:, 1, 0:E], before[:, :], routed[:, 0, :], start=True, stop=True)
            nc.tensor.matmul(ps[:, 1, E:2 * E], ones[:, :], routed[:, 0, :], start=True, stop=False)
            nc.tensor.matmul(ps[:, 1, E:2 * E], before[:, :], routed[:, 1, :], start=False, stop=True)
            nc.tensor.matmul(ps[:, 2, 0:E], ones[:, :], routed[:, 0, :], start=True, stop=False)
            nc.tensor.matmul(ps[:, 2, 0:E], ones[:, :], routed[:, 1, :], start=False, stop=True
                             ).then_inc(ranks_ps, 1)

            def gather(p, g):
                pe.wait_ge(picked_s, p + 1)
                wait(pe, x_sb, 2 * p + g)
                for c in range(8):
                    for t in range(TT):
                        mm = nc.tensor.matmul(ps_x[:, c // 4, (c % 4) * P:(c % 4 + 1) * P],
                                              h[:, t, g * 1024 + c:(g + 1) * 1024:8],
                                              pick[:, t, :, :].rearrange("p i s -> p (i s)"),
                                              start=(t == 0), stop=(t == TT - 1))
                mm.then_inc(x_ps, 1)

            def chunk_landed(j, n):
                s = slot_of(j)
                pe.wait_ge(arrived[s], 16 * (used_before(s) + n) + 16)
                return s

            def pair(i):
                pe.wait_ge(x_sb, 2 * i + 2)
                for q in range(2):
                    n = 2 * i + q
                    wait(pe, act_done, n)
                    wait(pe, mid_done, n)
                    for j in range(0, 8, 2):
                        kind, g, c0 = CHUNKS[j]
                        s = chunk_landed(j, n)
                        chunk_landed(j + 1, n)
                        for c in range(4):
                            for hh in range(2):
                                mm = nc.tensor.matmul(
                                    ps_gu[hh * SLOTS:(hh + 1) * SLOTS, :].rearrange("p (a f) -> p a f", a=2),
                                    xgT[:, g * 8 + c0 + c, q, :],
                                    ring[:, s:s + 2, c * FF + hh * 256:c * FF + (hh + 1) * 256],
                                    start=(j == 0 and c == 0), stop=(j == 6 and c == 3))
                        mm.then_inc(freed[s + 1], 1)
                    if q == 0:
                        pe.wait_ge(weighted, i + 1)
                        wait(pe, pT_sb, i)
                        for t in range(TT):
                            mm = nc.tensor.transpose(ps_pT[:, t * P:(t + 1) * P],
                                                     pick_w[:, t, :, :].rearrange("p i s -> p (i s)"), ident[:, :])
                        mm.then_inc(pT_ps, 1)
                    else:
                        gather(i + 1, 0)
                    pe.wait_ge(mid_done, n + 1)
                    wait(pe, midT_sb, n)
                    for c in range(2):
                        mm = nc.tensor.transpose(ps_mid[:, c * P:(c + 1) * P], mid[:, c * P:(c + 1) * P], ident[:, :])
                    mm.then_inc(midT_ps, 1)
                    pe.wait_ge(midT_sb, n + 1)
                    wait(pe, y_sb[0], n)
                    wait(pe, y_sb[1], n)
                    for f in range(4):
                        s = chunk_landed(8 + f, n)
                        for nb in range(2):
                            for g in range(2):
                                mm = nc.tensor.matmul(ps_y[g * SLOTS:(g + 1) * SLOTS, nb, :],
                                                      midT[:, f % 2, (f // 2) * SLOTS:(f // 2 + 1) * SLOTS],
                                                      ring[:, s, g * 1024 + nb * 512:g * 1024 + (nb + 1) * 512],
                                                      start=(f == 0), stop=(f == 3))
                        mm.then_inc(freed[s], 1)
                pe.wait_ge(y_sb[0], 2 * i + 2)
                pe.wait_ge(y_sb[1], 2 * i + 2)
                pe.wait_ge(pT_sb, i + 1)
                for t in range(TT):
                    for cb in range(4):
                        k = 4 * t + cb
                        wait(pe, added, 8 * i + k - 1)
                        nc.tensor.matmul(ps_add[:, k % 2, :], pickT[:, t, :], y[:, cb * 512:(cb + 1) * 512],
                                         start=True, stop=True).then_inc(add_ps, 1)
                gather(i + 1, 1)

            for g in range(2):
                gather(0, g)
            more_pairs = load_pairs(pe)
            item_loop(pe, pair, more_pairs)


def kernel(**inputs):
    import numpy as np
    import concourse.bacc as bacc
    from concourse import mybir as _mybir
    from concourse.bass_utils import run_bass_kernel_spmd

    inp = {n: np.asarray(a) for n, a in inputs.items()}
    tokens = np.concatenate([inp["meta_tokens"], inp["x"][0]], axis=0)
    tiles = [inp["conv_pw1_b"][0][:D].reshape(KT, P), inp["conv_pw1_b"][0][D:].reshape(KT, P),
             inp["conv_dw_b"][0].reshape(KT, P), inp["conv_ln_g"][0].reshape(KT, P), inp["conv_ln_b"][0].reshape(KT, P)]
    tiles += [tap.reshape(KT, P) for tap in inp["conv_dw_w"][0]]
    par = np.stack(tiles, axis=0).transpose(2, 1, 0).reshape(P, KT * PAR)
    rw = inp["router_w"].reshape(KT, P, E).transpose(1, 0, 2).reshape(P, KT * E)
    arrays = {
        "xT": tokens.T, "x": inp["x"][0], "par": par, "w1": inp["conv_pw1_w"][0], "w2": inp["conv_pw2_w"][0],
        "b2": inp["conv_pw2_b"], "ln1_g": inp["ln_mix_g"], "ln1_b": inp["ln_mix_b"],
        "ln2_g": inp["ln_ffn_g"], "ln2_b": inp["ln_ffn_b"], "rw": rw, "rb": inp["router_b"].reshape(1, E),
        "wg": inp["moe_w_gate"][0], "wu": inp["moe_w_up"][0], "wd": inp["moe_w_down"][0],
    }
    arrays = {f"in_{n}": np.ascontiguousarray(a) for n, a in arrays.items()}

    nc = bacc.Bacc("TRN2", target_bir_lowering=False, num_devices=1)
    args = [nc.dram_tensor(n, a.shape, _mybir.dt.from_np(a.dtype), kind="ExternalInput").ap()
            for n, a in arrays.items()]
    out = nc.dram_tensor("out", (SEQ, D), _mybir.dt.float32, kind="ExternalOutput").ap()
    build(nc, *args, out)
    result = run_bass_kernel_spmd(nc, [arrays], core_ids=[0])
    return result.results[0]["out"].reshape(1, SEQ, D)
```

```python
import concourse.bass as bass
from concourse import mybir
from concourse.bass import ds
from contextlib import ExitStack

D = 2048
SEQ = 256
META = 16
LEN = META + SEQ
TAPS = 31
E = 32
GROUPS = 4
PER = E // GROUPS
FF = 512
P = 128
KT = D // P
TT = SEQ // P
SLOTS = 64
BLOCKS = SEQ // SLOTS
ALPHA = 2.0 ** 0.25
LN_EPS = 1e-5
PAD = TAPS - 1 - META
PAR = 5 + TAPS
RING = 12
RAW = 4
PARTS = 4
W1_CHUNKS = 2 * KT
W_CHUNKS = W1_CHUNKS + KT
LOOKUPS = BLOCKS + 1
PW2_LEAD = 2
N_CONSTS = 9
TERMS = 17
ACT_TAPS = TERMS - 2
POOLED = 3
DVE_TAPS = TAPS - ACT_TAPS
TILE_OPS = 1 + DVE_TAPS + 1
TAP_OPS = 1 + 4 * TILE_OPS


def build(nc, xT_in, x_in, par_in, w1, w2, b2, ln1_g, ln1_b, ln2_g, ln2_b, rw_in, rb_in, wg, wu, wd, out):
    f32, bf16, u32, i32 = mybir.dt.float32, mybir.dt.bfloat16, mybir.dt.uint32, mybir.dt.int32
    f32r = mybir.dt.float32r
    ALU, ACT, AX = mybir.AluOpType, mybir.ActivationFunctionType, mybir.AxisListType

    ctx = ExitStack()
    with ctx:
        def sb(name, shape, dt=f32):
            return ctx.enter_context(nc.sbuf_tensor(name, shape, dt))

        def sem(name):
            return ctx.enter_context(nc.semaphore(name))

        def under(name, shape):
            with nc.sbuf_tensor(name, shape, f32r) as tensor:
                return tensor

        ring_r = under("ring_r", [P, RING, 2048])
        ring = sb("ring", [P, RING, 2048])
        xT_r = under("xT_r", [P, KT, LEN])
        x_lo = xT_r[:, :, :]
        s_hi = xT_r[:, :, 0:SEQ]
        xT = sb("xT", [P, KT, LEN])
        squares = xT[:, :, 0:SEQ]
        hT = xT[:, :, 0:SEQ]
        total = xT[:, :, 0:SEQ]
        s_lo = under("s_lo", [P, KT, SEQ])
        conv = sb("conv", [P, KT, SEQ])
        x_hi = under("x_hi", [P, KT, LEN])
        h = sb("h", [P, TT, D])
        gain = sb("gain", [P, D])
        bias = sb("bias", [P, D])
        par = sb("par", [P, KT * PAR])
        par_now = sb("par_now", [P, 4 * PAR])
        glu_sig = sb("glu_sig", [P, 2, LEN])
        u = sb("u", [P, 2, PAD + LEN])
        terms = sb("terms", [P, TERMS, SEQ])
        mean_sb, rstd_c, var_c, newton = (terms[:, m, :] for m in range(TERMS - 4, TERMS))
        minus_half = sb("minus_half", [P, 1])
        ones = sb("ones", [P, P])
        mean_w = sb("mean_w", [P, P])
        ident = sb("ident", [P, P])
        ident_alpha = sb("ident_alpha", [P, P])
        b2_row = bias[0:1, :]
        before = sb("before", [P, P], bf16)
        ones_b = sb("ones_b", [P, P], bf16)
        rw = sb("rw", [P, KT * E])
        logit_parts = mean_sb
        rb = sb("rb", [P, E])
        stats = sb("stats", [P, TT, 4, 6])
        mv = sb("mv", [P, TT, 2])
        rstd = sb("rstd", [P, TT])
        score = sb("score", [P, TT, E])
        sel = sb("sel", [P, TT, E])
        top8 = sb("top8", [P, TT, GROUPS, 8])
        gscore = sb("gscore", [P, TT, GROUPS])
        gbest = sb("gbest", [P, TT])
        gmark = sb("gmark", [P, TT, GROUPS])
        gfirst = sb("gfirst", [P, TT])
        grank = sb("grank", [P, GROUPS])
        sel_in = sb("sel_in", [P, TT, E])
        best = sb("best", [P, TT, 8])
        best_at = sb("best_at", [P, TT, 8], u32)
        best_f = sb("best_f", [P, TT, 2])
        hot = sb("hot", [P, 2, TT, E])
        gates = sb("gates", [P, 2, TT])
        gsum = sb("gsum", [P, TT])
        picked = sb("picked", [P, E])
        routed = sb("routed", [P, TT, E], bf16)
        rank = sb("rank", [P, TT, E])
        weight = sb("weight", [P, TT, E])
        expert_no = sb("expert_no", [P, E])
        most = sb("most", [P, 1])
        more = sb("more", [P, BLOCKS])
        pairs_f = sb("pairs_f", [P, 1])
        pairs_i = sb("pairs_i", [P, 1], i32)
        slot_no = sb("slot_no", [P, LOOKUPS, SLOTS])
        pick = sb("pick", [P, TT, 2, SLOTS])
        pick_w = sb("pick_w", [P, TT, 2, SLOTS])
        pickT = sb("pickT", [P, TT, P])
        y = conv[:, 0:8, :].rearrange("p k c -> p (k c)")
        xgT = conv[:, 8:16, :].rearrange("p k (a i s) -> p (k a) i s", a=2, i=2)
        act_sb, mid = terms[:, 0, :], terms[:, 1, :]
        midT = terms[:, 2, :].rearrange("p (c s) -> p c s", c=2)

        result = ring[:, 0:TT, :]

        ps = ctx.enter_context(nc.psum_tensor("ps", [P, 8, 512], f32))
        ps_gu, ps_mid, ps_pT = ps[:, 0, :], ps[:, 1, 0:256], ps[:, 1, 256:512]
        ps_y, ps_x, ps_add = ps[:, 2:4, :], ps[:, 4:6, :], ps[:, 6:8, :]

        arrived = [sem(f"arrived{s}") for s in range(RING)]
        freed = [sem(f"freed{s}") for s in range(RING)]
        xT_in_s = [sem("xT_lo"), sem("xT_hi")]
        par_s, x_s, b2_s, gain_s, bias_s, rw_s, rb_s = (
            sem(n) for n in ("par_in", "x_in", "b2_in", "gain_in", "bias_in", "rw_in", "rb_in"))
        consts = sem("consts")
        marks = sem("marks")
        x_hi_s, x_lo_s = sem("x_hi_s"), sem("x_lo_s")
        w_hi = sem("w_hi")
        w_lo = sem("w_lo")
        w_used = sem("w_used")
        primed = sem("primed")
        s_hi_s, s_lo_s = sem("s_hi_s"), sem("s_lo_s")
        glu_s = sem("glu_s")
        taps = sem("taps")
        pool_terms = sem("pool_terms")
        products = sem("products")
        pooled = sem("pooled")
        sums = sem("sums")
        centred = sem("centred")
        squared = sem("squared")
        var_in = sem("var_in")
        root = sem("root")
        var_ready = sem("var_ready")
        root_made = sem("root_made")
        scaled = sem("scaled")
        silu_c = sem("silu_c")
        pw2 = sem("pw2")
        step = sem("step")
        h_ready = sem("h_ready")
        hT_ps = sem("hT_ps")
        hT_sb = [sem("hT_sb_act"), sem("hT_sb_dve")]
        logits_T = sem("logits_T")
        logits = sem("logits")
        logit_sb = sem("logit_sb")
        logit_sum = sem("logit_sum")
        scores_s = sem("scores")
        routed_s = sem("routed_s")
        ranks_ps = sem("ranks_ps")
        pairs_s = sem("pairs_s")
        picked_s = sem("picked_s")
        weighted = sem("weighted")
        pT_ps = sem("pT_ps")
        pT_sb = sem("pT_sb")
        x_ps = sem("x_ps")
        x_sb = sem("x_sb")
        add_ps = sem("add_ps")
        added = sem("added")
        act_done = sem("act_done")
        mid_done = sem("mid_done")
        midT_ps = sem("midT_ps")
        midT_sb = sem("midT_sb")
        y_sb = [sem("y_sb_act"), sem("y_sb_dve")]
        all_added = sem("all_added")
        total_0 = sem("total_0")
        gain2_s, bias2_s = sem("gain2_in"), sem("bias2_in")
        out_ready = sem("out_ready")
        out_s = sem("out_s")

        block = ctx.enter_context(nc.Block())

        def wait(eng, s, value):
            if isinstance(value, int) and value <= 0:
                return
            eng.wait_ge(s, value)

        w1_v = w1.rearrange("(k p) n -> p k n", p=P)

        def raw_slot(n):
            return n % RAW

        def hi_slot(n):
            return RAW + 2 * (n % PARTS)

        def lo_slot(n):
            return RAW + 2 * (n % PARTS) + 1

        wg_v = wg.rearrange("e (g p c) n -> e g p (c n)", g=2, c=8)
        wu_v = wu.rearrange("e (g p c) n -> e g p (c n)", g=2, c=8)
        wd_v = wd.rearrange("e (f p) n -> e f p n", p=P)

        CHUNKS = []
        for g in range(2):
            for c0 in (0, 4):
                CHUNKS += [("gate", g, c0), ("up", g, c0)]
        CHUNKS += [("down", f, 0) for f in range(4)]

        def slot_of(j):
            return j % RING

        def landed_before(s):
            return W_CHUNKS // RAW if s < RAW else 0

        def chunk_used(eng, j, items):
            if not (isinstance(items, int) and items <= 0):
                eng.wait_ge(freed[slot_of(j)], items)

        def signal_of(j):
            return slot_of(j + 1 if CHUNKS[j][0] == "gate" else j)

        def n_is_first(n):
            return isinstance(n, int) and n == 0

        UP_END, DOWN_END = 7, 11

        def expert_of(m):
            return m % E

        def block_of(m):
            return m // E

        def item_loop(eng, body, more_pairs):
            body(0)
            with eng.Fori(1, E // 2) as i:
                body(i)
            with eng.If(more_pairs > E // 2):
                with eng.Fori(E // 2, more_pairs) as i:
                    body(i)

        def load_pairs(eng):
            eng.wait_ge(pairs_s, 1)
            return eng.value_load(pairs_i[0:1, 0:1], min_val=E // 2, max_val=BLOCKS * E // 2)

        @block.sync
        def _(sp):
            def pw1_chunks(i, xT_v=None):
                for c in range(8):
                    col = (c % 2) * D + (4 * i + c // 2) * P
                    wait(sp, w_lo, 8 * i + c - RAW + 1)
                    sp.dma_start(ring[:, raw_slot(c), :].rearrange("p (k n) -> p k n", k=KT),
                                 w1_v[:, :, ds(col, P)]).then_inc(arrived[raw_slot(c)], 16)
                    if xT_v is not None and c == 0:
                        sp.dma_start(xT[:, 8:16, :], xT_v[:, 8:16, :]).then_inc(xT_in_s[1], 16)
                        sp.dma_start(par[:, :], par_in).then_inc(par_s, 16)

            def pw2_chunk(k):
                n = W1_CHUNKS + k
                sp.wait_ge(w_lo, n - RAW + 1)
                sp.dma_start(ring[:, raw_slot(n), :], w2[k * P:(k + 1) * P, :]).then_inc(arrived[raw_slot(n)], 16)

            xT_v = xT_in.rearrange("(k p) t -> p k t", p=P)
            sp.dma_start(xT[:, 0:8, :], xT_v[:, 0:8, :]).then_inc(xT_in_s[0], 16)
            pw1_chunks(0, xT_v)
            sp.dma_start(b2_row, b2).then_inc(b2_s, 16)
            with sp.Fori(1, KT // 4) as i:
                pw1_chunks(i)
            for k in range(RAW):
                pw2_chunk(k)
            sp.wait_ge(w_used, W1_CHUNKS)
            sp.dma_start(h[:, :, :], x_in.rearrange("(t p) d -> p t d", p=P)).then_inc(x_s, 16)
            sp.dma_start(gain[:, :], ln1_g.broadcast_to([P, D])).then_inc(gain_s, 16)
            sp.dma_start(rw[:, :], rw_in).then_inc(rw_s, 16)
            sp.dma_start(rb[:, :], rb_in.broadcast_to([P, E])).then_inc(rb_s, 16)
            for k in range(RAW, KT):
                pw2_chunk(k)
                if k == RAW + 3:
                    sp.wait_ge(primed, 1)
                    sp.dma_start(bias[:, :], ln1_b.broadcast_to([P, D])).then_inc(bias_s, 16)

            def expert_chunks(n):
                e = expert_of(n)
                for j, (kind, a, c0) in enumerate(CHUNKS):
                    s = slot_of(j)
                    if n_is_first(n) and s < RAW:
                        sp.wait_ge(w_lo, W_CHUNKS - RAW + s + 1)
                    elif n_is_first(n):
                        sp.wait_ge(w_used, W_CHUNKS - PARTS + (s - RAW) // 2 + 1)
                    else:
                        sp.wait_ge(freed[signal_of(j)], n)
                    if kind == "down":
                        src = wd_v[ds(e, 1), a, :, :].rearrange("o p n -> (o p) n")
                    else:
                        src = (wg_v if kind == "gate" else wu_v)[ds(e, 1), a, :, c0 * FF:(c0 + 4) * FF]\
                            .rearrange("o p n -> (o p) n")
                    sp.dma_start(ring[:, s, :], src).then_inc(arrived[s], 16)

            def pair(i):
                for q in range(2):
                    expert_chunks(2 * i + q)

            pair(0)
            sp.wait_ge(h_ready, 4 * TT)
            sp.dma_start(gain[:, :], ln2_g.broadcast_to([P, D])).then_inc(gain2_s, 16)
            sp.dma_start(bias[:, :], ln2_b.broadcast_to([P, D])).then_inc(bias2_s, 16)
            more_pairs = load_pairs(sp)
            with sp.Fori(1, E // 2) as i:
                pair(i)
            with sp.If(more_pairs > E // 2):
                with sp.Fori(E // 2, more_pairs) as i:
                    pair(i)

            sp.wait_ge(out_ready, 4)
            sp.dma_start(out[0:P, :], result[:, 0, :]).then_inc(out_s, 16)
            for c in range(4):
                cols = slice(c * 512, (c + 1) * 512)
                sp.wait_ge(out_ready, 4 + c + 1)
                sp.dma_start(out[P:2 * P, cols], result[:, 1, cols]).then_inc(out_s, 16)
            sp.wait_ge(out_s, 16 * 5)

        @block.gpsimd
        def _(pool):
            n_marks = [0]

            def mark(ins):
                n_marks[0] += 1
                ins.then_inc(marks, 1)
                pool.wait_ge(marks, n_marks[0])

            def const(ins):
                ins.then_inc(consts, 1)

            mark(nc.gpsimd.memset(minus_half[:, :], -0.5))
            const(nc.gpsimd.memset(ones[:, :], 1.0))
            const(nc.gpsimd.memset(ones_b[:, :], 1.0))
            const(nc.gpsimd.memset(mean_w[:, :], 1.0 / D))
            mark(nc.gpsimd.memset(ident[:, :], 0.0))
            const(nc.gpsimd.affine_select(out=ident[:, :], in_=ident[:, :], compare_op=ALU.not_equal, fill=1.0,
                                         base=0, pattern=[[-1, P]], channel_multiplier=1))
            mark(nc.gpsimd.memset(ident_alpha[:, :], 0.0))
            const(nc.gpsimd.affine_select(out=ident_alpha[:, :], in_=ident_alpha[:, :], compare_op=ALU.not_equal,
                                         fill=ALPHA, base=0, pattern=[[-1, P]], channel_multiplier=1))
            mark(nc.gpsimd.memset(before[:, :], 0.0))
            const(nc.gpsimd.affine_select(out=before[:, :], in_=before[:, :], compare_op=ALU.is_ge, fill=1.0,
                                         base=0, pattern=[[-1, P]], channel_multiplier=1))
            fl = dict(allow_small_or_imprecise_dtypes=True)
            const(nc.gpsimd.iota(expert_no[:, :], [[1, E]], base=0, channel_multiplier=0, **fl))
            const(nc.gpsimd.iota(grank[:, :], [[-1, GROUPS]], base=GROUPS, channel_multiplier=0, **fl))
            const(nc.gpsimd.iota(slot_no[:, :, :], [[SLOTS, LOOKUPS], [1, SLOTS]], base=0,
                                 channel_multiplier=0, **fl))

            def low(n, c):
                pool.wait_ge(w_hi, n + 1)
                nc.gpsimd.tensor_tensor(ring_r[:, lo_slot(c), :], ring[:, raw_slot(c), :],
                                        ring_r[:, hi_slot(c), :].bitcast(f32), ALU.subtract).then_inc(w_lo, 1)

            def pool_sum(tile):
                pool.wait_ge(pool_terms, tile + 1)
                first, last = terms[:, 2:2 + POOLED, :], terms[:, TERMS - POOLED:TERMS, :]
                nc.gpsimd.tensor_tensor(first, first, last, ALU.add).then_inc(pooled, 1)

            def low_pass(i):
                for j in range(4):
                    low(8 * i + 2 * j + PARTS, 2 * j % 4)
                    pool_sum(4 * i + j)
                    low(8 * i + 2 * j + 1 + PARTS, (2 * j + 1) % 4)

            def inverse_root(count, dst, var):
                pool.wait_ge(var_ready, count)
                nc.gpsimd.tensor_tensor(dst, var, minus_half[:, 0:1], ALU.pow).then_inc(root_made, 1)

            for n in range(PARTS):
                low(n, n)
            with pool.Fori(0, KT // 4) as i:
                low_pass(i)
            for n in range(W1_CHUNKS + PARTS, W_CHUNKS):
                low(n, n % 4)
            for norm in range(2):
                for t in range(TT):
                    inverse_root(1 + norm * TT + t, rstd[:, t:t + 1], mv[:, t, 1:2])

        @block.scalar
        def _(act):
            def preload(func):
                act.preload_act_table(func)

            def high(n, c):
                act.wait_ge(arrived[raw_slot(c)], 16 * (n - c) // RAW + 16 * (c // RAW) + 16)
                wait(act, w_used, n - PARTS + 1)
                nc.scalar.activation(ring_r[:, hi_slot(c), :], ring[:, raw_slot(c), :], ACT.Copy
                                     ).then_inc(w_hi, 1)

            preload(ACT.Sigmoid)
            for half in range(2):
                act.wait_ge(xT_in_s[half], 16)
                nc.scalar.activation(x_hi[:, 8 * half:8 * half + 8, :], xT[:, 8 * half:8 * half + 8, :], ACT.Copy
                                     ).then_inc(x_hi_s, 1)
                high(half, half)
            for n in range(2, PARTS):
                high(n, n)

            act.wait_ge(par_s, 16)

            def gates_of(i):
                for j in range(4):
                    high(8 * i + 2 * j + PARTS, 2 * j + PARTS)
                    act.wait_ge(w_used, 8 * i + 2 * j + 2)
                    if j < 2:
                        wait(act, taps, (i - 1) * TAP_OPS + 1 + (j + 2) * TILE_OPS + 1)
                    else:
                        act.wait_ge(taps, i * TAP_OPS + 1 + (j - 2) * TILE_OPS + 1)
                    nc.scalar.activation(glu_sig[:, j % 2, :], ps[:, 2 * j + 1, 0:LEN], ACT.Sigmoid,
                                         bias=par[:, ds((4 * i + j) * PAR + 1, 1)]).then_inc(glu_s, 1)
                    high(8 * i + 2 * j + 1 + PARTS, 2 * j + 1 + PARTS)
                    act.wait_ge(taps, i * TAP_OPS + 1 + j * TILE_OPS + 1)
                    order = list(range(2, 2 + POOLED)) + list(range(TERMS - POOLED, TERMS)) \
                        + list(range(2 + POOLED, TERMS - POOLED))
                    for at, m in enumerate(order):
                        k = DVE_TAPS + m - 2
                        ins = nc.scalar.activation(terms[:, m, :], u[:, j % 2, k:k + SEQ], ACT.Copy,
                                                   scale=par[:, ds((4 * i + j) * PAR + 5 + k, 1)])
                        if at == 2 * POOLED - 1:
                            ins.then_inc(pool_terms, 1)
                    ins.then_inc(products, 1)

            gates_of(0)
            with act.Fori(1, KT // 4) as i:
                gates_of(i)

            for c in range(4):
                act.wait_ge(centred, c + 1)
                nc.scalar.activation(squares[:, 4 * c:4 * c + 4, :], conv[:, 4 * c:4 * c + 4, :], ACT.Square
                                     ).then_inc(squared, 1)
            preload(ACT.Sqrt)
            act.wait_ge(var_in, 1)
            nc.scalar.activation(rstd_c, var_c, ACT.Sqrt).then_inc(root, 1)
            preload(ACT.Silu)
            for k in range(KT):
                act.wait_ge(scaled, k // 4 + 1)
                nc.scalar.activation(conv[:, k, :], conv[:, k, :], ACT.Silu,
                                     scale=par[:, k * PAR + 3:k * PAR + 4],
                                     bias=par[:, k * PAR + 4:k * PAR + 5]).then_inc(silu_c, 1)
            for n in range(W1_CHUNKS + PARTS, W_CHUNKS):
                high(n, n)
            for n in range(3):
                t, half = n // 2, n % 2
                if n == 2:
                    act.wait_ge(logits, 1)
                    nc.scalar.activation(logit_parts[:, 0:P], ps[:, 0, 0:P], ACT.Copy).then_inc(logit_sb, 1)
                act.wait_ge(hT_ps, n + 1)
                nc.scalar.activation(hT[:, 8 * half:8 * half + 8, t * P:(t + 1) * P],
                                     ps[:, 4 * t + 2 * half:4 * t + 2 * half + 2, :]
                                     .rearrange("p b (k c) -> p (b k) c", c=P), ACT.Copy).then_inc(hT_sb[0], 1)
            preload(ACT.Sigmoid)
            act.wait_ge(logit_sum, 1)
            nc.scalar.activation(score[:, :, :], score[:, :, :], ACT.Sigmoid).then_inc(scores_s, 1)
            more_pairs = load_pairs(act)

            preload(ACT.Silu)

            def copy_x(p, g):
                act.wait_ge(x_ps, 2 * p + g + 1)
                chunk_used(act, UP_END, 2 * p)
                nc.scalar.activation(xgT[:, 8 * g:8 * g + 8, :, :], (ps_x, ps_add)[g].rearrange(
                    "p b (k i s) -> p (b k) i s", i=2, s=SLOTS), ACT.Copy).then_inc(x_sb, 1)

            def pair(i):
                for q in range(2):
                    n = 2 * i + q
                    chunk_used(act, UP_END, n + 1)
                    wait(act, mid_done, n)
                    nc.scalar.activation(act_sb, ps_gu[:, 0:256], ACT.Silu).then_inc(act_done, 1)
                    chunk_used(act, DOWN_END, n + 1)
                    wait(act, add_ps, 8 * i)
                    nc.scalar.activation(y[q * SLOTS:(q + 1) * SLOTS, 0:1024],
                                         ps_y[0:SLOTS, :, :].rearrange("p b n -> p (b n)"), ACT.Copy
                                         ).then_inc(y_sb[0], 1)
                for g in range(2):
                    copy_x(i + 1, g)

            for g in range(2):
                copy_x(0, g)
            pair(0)
            with act.Fori(1, E // 2) as i:
                pair(i)
            with act.If(more_pairs > E // 2):
                with act.Fori(E // 2, more_pairs) as i:
                    pair(i)

        @block.vector
        def _(dve):
            n_step, n_root = [0], [0]

            def done(ins):
                n_step[0] += 1
                ins.then_inc(step, 1)
                dve.wait_ge(step, n_step[0])

            def inverse_root(root, var, tmp):
                n_root[0] += 1
                dve.wait_ge(root_made, n_root[0])
                refine(root, var, tmp)

            def refine(root, var, tmp):
                done(nc.vector.tensor_tensor(tmp, root, root, ALU.mult))
                done(nc.vector.tensor_tensor(tmp, tmp, var, ALU.mult))
                done(nc.vector.tensor_scalar(tmp, tmp, -0.5, 1.5, ALU.mult, ALU.add))
                done(nc.vector.tensor_tensor(root, root, tmp, ALU.mult))

            done(nc.vector.memset(u[:, :, 0:PAD], 0.0))
            for half in range(2):
                dve.wait_ge(x_hi_s, half + 1)
                part = slice(8 * half, 8 * half + 8)
                nc.vector.tensor_tensor(x_lo[:, part, :], xT[:, part, :], x_hi[:, part, :].bitcast(f32),
                                        ALU.subtract).then_inc(x_lo_s, 1)
            dve.wait_ge(par_s, 16)

            def conv_pass(i):
                base = i * TAP_OPS
                wait(dve, taps, base)
                nc.vector.tensor_copy(par_now[:, :], par[:, ds(4 * i * PAR, 4 * PAR)]).then_inc(taps, 1)
                for j in range(4):
                    count = base + 1 + j * TILE_OPS
                    dve.wait_ge(taps, count)
                    dve.wait_ge(glu_s, 4 * i + j + 1)
                    nc.vector.scalar_tensor_tensor(
                        out=u[:, j % 2, PAD:PAD + LEN], in0=ps[:, 2 * j, 0:LEN],
                        scalar=par_now[:, j * PAR:j * PAR + 1], in1=glu_sig[:, j % 2, :],
                        op0=ALU.add, op1=ALU.mult).then_inc(taps, 1)
                    dve.wait_ge(taps, count + 1)
                    for k in range(DVE_TAPS):
                        tap = par_now[:, j * PAR + 5 + k:j * PAR + 6 + k]
                        src, dst = u[:, j % 2, k:k + SEQ], terms[:, k % 2, :]
                        if k == 0:
                            ins = nc.vector.tensor_scalar(dst, src, tap, par_now[:, j * PAR + 2:j * PAR + 3],
                                                          ALU.mult, ALU.add)
                        elif k == 1:
                            ins = nc.vector.tensor_scalar(dst, src, tap, None, ALU.mult)
                        else:
                            dve.wait_ge(taps, count + k)
                            ins = nc.vector.scalar_tensor_tensor(out=dst, in0=src, scalar=tap, in1=dst,
                                                                 op0=ALU.mult, op1=ALU.add)
                        ins.then_inc(taps, 1)
                    dve.wait_ge(taps, count + 1 + DVE_TAPS)
                    dve.wait_ge(products, 4 * i + j + 1)
                    dve.wait_ge(pooled, 4 * i + j + 1)
                    nc.vector.tensor_reduce(conv[:, ds(4 * i + j, 1), :].rearrange("p o t -> p (o t)"),
                                            terms[:, 0:TERMS - POOLED, :].rearrange("p m t -> p t m"),
                                            AX.X, ALU.add
                                            ).then_inc(taps, 1)

            conv_pass(0)
            with dve.Fori(1, 4) as i:
                conv_pass(i)

            dve.wait_ge(sums, 1)
            done(nc.vector.tensor_copy(mean_sb, ps[:, 6, 0:SEQ]))
            for c in range(4):
                part = conv[:, 4 * c:4 * c + 4, :]
                nc.vector.tensor_tensor(part, part, mean_sb.rearrange("p (o t) -> p o t", o=1)
                                        .broadcast_to([P, 4, SEQ]), ALU.subtract).then_inc(centred, 1)
            dve.wait_ge(sums, 2)
            nc.vector.tensor_scalar(var_c, ps[:, 7, 0:SEQ], LN_EPS, None, ALU.add).then_inc(var_in, 1)
            dve.wait_ge(root, 1)
            done(nc.vector.reciprocal(rstd_c, rstd_c))
            refine(rstd_c, var_c, newton)
            def split_tiles(c):
                dve.wait_ge(silu_c, 4 * c + 4)
                part = slice(4 * c, 4 * c + 4)
                nc.vector.tensor_copy(s_hi[:, part, :], conv[:, part, :]).then_inc(s_hi_s, 1)
                dve.wait_ge(s_hi_s, c + 1)
                nc.vector.tensor_tensor(s_lo[:, part, :], conv[:, part, :], s_hi[:, part, :].bitcast(f32),
                                        ALU.subtract).then_inc(s_lo_s, 1)

            for c in range(4):
                part = conv[:, 4 * c:4 * c + 4, :]
                nc.vector.tensor_tensor(part, part, rstd_c.rearrange("p (o t) -> p o t", o=1)
                                        .broadcast_to([P, 4, SEQ]), ALU.mult).then_inc(scaled, 1)
                if c > 0:
                    split_tiles(c - 1)
            split_tiles(3)

            def norm_stats(t, src, bank_done=None):
                for c in range(4):
                    if bank_done:
                        bank_done(c)
                    ins = nc.vector.bn_stats(stats[:, t, c, :], src[:, c])
                done(ins)
                done(nc.vector.bn_aggr(mv[:, t, :], stats[:, t, :, :].rearrange("p c s -> p (c s)")))
                nc.vector.tensor_scalar(mv[:, t, 1:2], mv[:, t, 1:2], LN_EPS, None, ALU.add).then_inc(var_ready, 1)
                inverse_root(rstd[:, t:t + 1], mv[:, t, 1:2], newton[:, 0:1])

            def norm_apply(t, ready, src, dst):
                first = []
                for c in range(5):
                    if c < 4:
                        cols = slice(c * 512, (c + 1) * 512)
                        gain_c = gain[:, cols]
                        dst_c = dst[:, cols]
                        if len(src.shape) == 4:
                            gain_c, dst_c = (a.rearrange("p (j c) -> p j c", c=src.shape[3]) for a in (gain_c, dst_c))
                        nc.vector.scalar_tensor_tensor(out=dst_c, in0=src[:, c], scalar=mv[:, t, 0:1], in1=gain_c,
                                                       op0=ALU.subtract, op1=ALU.mult).then_inc(step, 1)
                        n_step[0] += 1
                        first.append(n_step[0])
                    if c > 0:
                        cols = slice((c - 1) * 512, c * 512)
                        dve.wait_ge(step, first[c - 1])
                        nc.vector.scalar_tensor_tensor(out=dst[:, cols], in0=dst[:, cols], scalar=rstd[:, t:t + 1],
                                                       in1=bias[:, cols], op0=ALU.mult, op1=ALU.add
                                                       ).then_inc(ready, 1)

            dve.wait_ge(gain_s, 16)
            dve.wait_ge(bias_s, 16)
            for t in range(TT):
                def bank_done(c):
                    if 4 * t + c < 7:
                        dve.wait_ge(pw2, 4 * t + c + 1)
                    else:
                        dve.wait_ge(w_used, W_CHUNKS)

                norm_stats(t, ps[:, 4 * t:4 * t + 4, :], bank_done)
                norm_apply(t, h_ready, ps[:, 4 * t:4 * t + 4, :], h[:, t, :])
            dve.wait_ge(hT_ps, 2 * TT)
            nc.vector.tensor_copy(hT[:, 8:16, P:2 * P], ps[:, 6:8, :].rearrange("p b (k c) -> p (b k) c", c=P)
                                  ).then_inc(hT_sb[1], 1)

            dve.wait_ge(logits, 2)
            nc.vector.tensor_copy(logit_parts[:, P:2 * P], ps[:, 1, 0:P]).then_inc(logit_sb, 1)
            dve.wait_ge(logits_T, 1)
            nc.vector.tensor_reduce(score[:, :, :], ps[:, 2, 0:SEQ].rearrange("p (t g e) -> p t e g", t=TT, g=4),
                                    AX.X, ALU.add).then_inc(logit_sum, 1)

            dve.wait_ge(consts, N_CONSTS)
            dve.wait_ge(rb_s, 16)
            dve.wait_ge(scores_s, 1)
            rb_b = rb[:, :].rearrange("p (o e) -> p o e", o=1).broadcast_to([P, TT, E])
            done(nc.vector.tensor_tensor(sel[:, :, :], score[:, :, :], rb_b, ALU.add))
            for t in range(TT):
                for g in range(GROUPS):
                    ins = nc.vector.max(top8[:, t, g, :], sel[:, t, g * PER:(g + 1) * PER])
            done(ins)
            done(nc.vector.tensor_tensor(gscore[:, :, :], top8[:, :, :, 0], top8[:, :, :, 1], ALU.add))
            done(nc.vector.tensor_reduce(gbest[:, :], gscore[:, :, :], AX.X, ALU.max))
            gb = gbest[:, :].rearrange("p (t o) -> p t o", o=1).broadcast_to([P, TT, GROUPS])
            gr = grank[:, :].rearrange("p (o g) -> p o g", o=1).broadcast_to([P, TT, GROUPS])
            done(nc.vector.tensor_tensor(gmark[:, :, :], gscore[:, :, :], gb, ALU.is_equal))
            done(nc.vector.tensor_tensor(gmark[:, :, :], gmark[:, :, :], gr, ALU.mult))
            done(nc.vector.tensor_reduce(gfirst[:, :], gmark[:, :, :], AX.X, ALU.max))
            gf = gfirst[:, :].rearrange("p (t o) -> p t o", o=1).broadcast_to([P, TT, GROUPS])
            done(nc.vector.tensor_tensor(gmark[:, :, :], gr, gf, ALU.is_equal))
            done(nc.vector.tensor_scalar(gmark[:, :, :], gmark[:, :, :], -1.0, 1e30, ALU.add, ALU.mult))
            for t in range(TT):
                ins = nc.vector.tensor_tensor(
                    sel_in[:, t, :].rearrange("p (g e) -> p g e", g=GROUPS),
                    sel[:, t, :].rearrange("p (g e) -> p g e", g=GROUPS),
                    gmark[:, t, :].rearrange("p (g o) -> p g o", o=1).broadcast_to([P, GROUPS, PER]), ALU.add)
            done(ins)
            for t in range(TT):
                done(nc.vector.max(best[:, t, :], sel_in[:, t, :]))
                done(nc.vector.max_index(best_at[:, t, :], best[:, t, :], sel_in[:, t, :]))
            done(nc.vector.tensor_copy(best_f[:, :, :], best_at[:, :, 0:2]))
            no_b = expert_no[:, :].rearrange("p (o e) -> p o e", o=1).broadcast_to([P, TT, E])
            for k in range(2):
                ins = nc.vector.tensor_tensor(hot[:, k, :, :], no_b,
                                              best_f[:, :, k:k + 1].broadcast_to([P, TT, E]), ALU.is_equal)
            done(ins)
            nc.vector.tensor_tensor(routed[:, :, :], hot[:, 0, :, :], hot[:, 1, :, :], ALU.add
                                    ).then_inc(routed_s, 1)
            dve.wait_ge(routed_s, 1)
            dve.wait_ge(ranks_ps, 1)
            ps_rank = ps[:, 2, 0:TT * E].rearrange("p (t e) -> p t e", t=TT)
            done(nc.vector.scalar_tensor_tensor(out=rank[:, :, :], in0=ps_rank, scalar=1.0,
                                                in1=routed[:, :, :], op0=ALU.add, op1=ALU.mult))
            done(nc.vector.tensor_scalar(rank[:, :, :], rank[:, :, :], -1.0, None, ALU.add))
            def pick_slots(p):
                wait(dve, x_ps, 2 * p)
                wait(dve, weighted, p)
                nc.vector.tensor_tensor(
                    pick[:, :, :, :],
                    slot_no[:, ds(block_of(2 * p), 1), :].rearrange("p (o i) s -> p o i s", o=1)
                    .broadcast_to([P, TT, 2, SLOTS]),
                    rank[:, :, ds(expert_of(2 * p), 2)].rearrange("p t (i o) -> p t i o", o=1)
                    .broadcast_to([P, TT, 2, SLOTS]), ALU.is_equal).then_inc(picked_s, 1)

            pick_slots(0)
            done(nc.vector.reduce_max(most[:, :], ps[:, 3, 0:E], AX.X))
            nc.vector.memset(more[:, 0:1], E / 2.0)
            for b in range(1, BLOCKS):
                ins = nc.vector.tensor_scalar(more[:, b:b + 1], most[:, :], float(b * SLOTS), E / 2.0,
                                              ALU.is_gt, ALU.mult)
            done(ins)
            done(nc.vector.reduce_sum(pairs_f[:, :], more[:, :], AX.X))
            nc.vector.tensor_copy(pairs_i[:, :], pairs_f[:, :]).then_inc(pairs_s, 1)
            for k in range(2):
                for t in range(TT):
                    nc.vector.tensor_tensor_reduce(out=picked[:, :], in0=score[:, t, :], in1=hot[:, k, t, :],
                                                   scale=1.0, scalar=0.0, op0=ALU.mult, op1=ALU.add,
                                                   accum_out=gates[:, k, t:t + 1]).then_inc(step, 1)
                    n_step[0] += 1
                    dve.wait_ge(step, n_step[0])
            done(nc.vector.tensor_tensor(gsum[:, :], gates[:, 0, :], gates[:, 1, :], ALU.add))
            done(nc.vector.reciprocal(gsum[:, :], gsum[:, :]))
            for k in range(2):
                ins = nc.vector.tensor_tensor(gates[:, k, :], gates[:, k, :], gsum[:, :], ALU.mult)
            done(ins)
            for t in range(TT):
                done(nc.vector.tensor_scalar(weight[:, t, :], hot[:, 0, t, :], gates[:, 0, t:t + 1], None, ALU.mult))
                done(nc.vector.scalar_tensor_tensor(out=weight[:, t, :], in0=hot[:, 1, t, :],
                                                    scalar=gates[:, 1, t:t + 1], in1=weight[:, t, :],
                                                    op0=ALU.mult, op1=ALU.add))
            more_pairs = load_pairs(dve)

            def pair(i):
                dve.wait_ge(picked_s, i + 1)
                wait(dve, pT_ps, i)
                nc.vector.tensor_tensor(
                    pick_w[:, :, :, :], pick[:, :, :, :],
                    weight[:, :, ds(expert_of(2 * i), 2)].rearrange("p t (i o) -> p t i o", o=1)
                    .broadcast_to([P, TT, 2, SLOTS]), ALU.mult).then_inc(weighted, 1)
                pick_slots(i + 1)
                if isinstance(i, int):
                    nc.vector.tensor_scalar(total.rearrange("p (t j) c -> p t j c", t=TT),
                                            h[:, :, :].rearrange("p t (j c) -> p t j c", c=SEQ),
                                            ALPHA, None, ALU.mult).then_inc(total_0, 1)
                for q in range(2):
                    n = 2 * i + q
                    dve.wait_ge(act_done, n + 1)
                    wait(dve, midT_ps, n)
                    nc.vector.tensor_tensor(mid, act_sb, ps_gu[:, 256:512], ALU.mult).then_inc(mid_done, 1)
                    dve.wait_ge(midT_ps, n + 1)
                    chunk_used(dve, DOWN_END, n)
                    nc.vector.tensor_copy(midT, ps_mid.rearrange("p (c s) -> p c s", c=2)).then_inc(midT_sb, 1)
                    if q == 0:
                        dve.wait_ge(pT_ps, i + 1)
                        wait(dve, add_ps, 8 * i)
                        nc.vector.tensor_copy(pickT[:, :, :], ps_pT.rearrange("p (t c) -> p t c", t=TT)
                                              ).then_inc(pT_sb, 1)
                    chunk_used(dve, DOWN_END, n + 1)
                    wait(dve, add_ps, 8 * i)
                    nc.vector.tensor_copy(y[q * SLOTS:(q + 1) * SLOTS, 1024:2048],
                                          ps_y[SLOTS:P, :, :].rearrange("p b n -> p (b n)")).then_inc(y_sb[1], 1)
                if isinstance(i, int):
                    dve.wait_ge(total_0, 1)
                for t in range(TT):
                    for cb in range(4):
                        k = 4 * t + cb
                        dve.wait_ge(add_ps, 8 * i + k + 1)
                        part = total[:, 2 * k:2 * k + 2, :]
                        nc.vector.tensor_tensor(part, part,
                                                ps_add[:, k % 2, :].rearrange("p (j c) -> p j c", j=2),
                                                ALU.add).then_inc(added, 1)

            pair(0)
            with dve.Fori(1, E // 2) as i:
                pair(i)
            with dve.If(more_pairs > E // 2):
                with dve.Fori(E // 2, more_pairs) as i:
                    pair(i)
            dve.drain().then_inc(all_added, 1)
            dve.wait_ge(all_added, 1)

            dve.wait_ge(gain2_s, 16)
            dve.wait_ge(bias2_s, 16)
            for t in range(TT):
                src = total[:, 8 * t:8 * t + 8, :].rearrange("p (c a) n -> p c a n", c=4)
                norm_stats(t, src)
                norm_apply(t, out_ready, src, result[:, t, :])

        @block.tensor
        def _(pe):
            def pw1_pass(i):
                for c in range(8):
                    j = c // 2
                    first = isinstance(i, int) and c == 0
                    if c % 2 == 0:
                        wait(pe, taps, (i - 1) * TAP_OPS + 1 + j * TILE_OPS + 1)
                    else:
                        wait(pe, glu_s, 4 * (i - 1) + j + 1)
                    w_parts = [ring_r[:, s, :].rearrange("p (k n) -> p k n", k=KT) for s in (hi_slot(c), lo_slot(c))]
                    n = 8 * i + c
                    for part, (w_part, x_part) in enumerate(((0, x_hi), (0, x_lo), (1, x_hi))):
                        if part == 0:
                            pe.wait_ge(w_hi, n + 1)
                        if part == 2:
                            pe.wait_ge(w_lo, n + 1)
                        for k in range(KT):
                            if first and part < 2 and k % 8 == 0:
                                pe.wait_ge((x_hi_s, x_lo_s)[part], k // 8 + 1)
                            mm = nc.tensor.matmul(ps[:, c, 0:LEN], w_parts[w_part][:, k, :], x_part[:, k, :],
                                                  start=(part == 0 and k == 0), stop=(part == 2 and k == KT - 1))
                    mm.then_inc(w_used, 1)

            pw1_pass(0)
            with pe.Fori(1, KT // 4) as i:
                pw1_pass(i)

            def prime_bias(bank):
                nc.tensor.matmul(ps[:, bank, :], ones[0:1, :], b2_row[:, bank % 4 * 512:(bank % 4 + 1) * 512],
                                 start=True, stop=False)

            def prime_x(bank):
                return nc.tensor.matmul(ps[:, bank, :], ident_alpha[:, :],
                                        h[:, bank // 4, bank % 4 * 512:(bank % 4 + 1) * 512], start=False, stop=False)

            def mean_part(k):
                pe.wait_ge(taps, (k // 4) * TAP_OPS + 1 + (k % 4 + 1) * TILE_OPS)
                return nc.tensor.matmul(ps[:, 6, 0:SEQ], mean_w[:, :], conv[:, k, :], start=(k == 0),
                                        stop=(k == KT - 1))

            pe.wait_ge(consts, N_CONSTS)
            pe.wait_ge(b2_s, 16)
            pe.wait_ge(taps, 3 * TAP_OPS + 1 + 2 * TILE_OPS + 1)
            for bank in range(6):
                prime_bias(bank)
            pe.wait_ge(taps, 3 * TAP_OPS + 1 + 3 * TILE_OPS + 1)
            for k in range(KT - 1):
                mean_part(k)
            pe.wait_ge(x_s, 16)
            for bank in range(1):
                prime_x(bank)
            mean_part(KT - 1).then_inc(sums, 1)
            for bank in range(1, 3):
                prime_x(bank)
            for k in range(KT):
                if k % 4 == 0:
                    pe.wait_ge(squared, k // 4 + 1)
                mm = nc.tensor.matmul(ps[:, 7, 0:SEQ], mean_w[:, :], squares[:, k, :], start=(k == 0),
                                      stop=(k == KT - 1))
            mm.then_inc(sums, 1)
            for bank in range(3, 6):
                prime_x(bank)
            pe.wait_ge(var_in, 1)
            for bank in range(6, 8):
                prime_bias(bank)
                mm = prime_x(bank)
            mm.then_inc(primed, 1)

            def pw2_part(t, k):
                n = W1_CHUNKS + k
                parts = ((s_hi, hi_slot(n)), (s_lo, hi_slot(n)), (s_hi, lo_slot(n)))
                order = [(part, nb) for nb in range(4) for part in range(3)] if k == KT - 1 \
                    else [(part, nb) for part in range(3) for nb in range(4)]
                for at, (part, nb) in enumerate(order):
                    if t == 0 and k % 4 == 0 and (part, nb) == (1, 0):
                        pe.wait_ge(s_lo_s, k // 4 + 1)
                    if t == 0 and (part, nb) == (2, 0):
                        pe.wait_ge(w_lo, n + 1)
                    s_part, slot = parts[part]
                    mm = nc.tensor.matmul(ps[:, 4 * t + nb, :], s_part[:, k, t * P:(t + 1) * P],
                                          ring_r[:, slot, nb * 512:(nb + 1) * 512],
                                          start=False, stop=(k == KT - 1 and part == 2))
                    if k == KT - 1 and part == 2 and at < len(order) - (1 if t == 1 else 0):
                        mm.then_inc(pw2, 1)
                return mm

            for step_k in range(KT + PW2_LEAD):
                if step_k < KT:
                    k = step_k
                    if k % 4 == 0:
                        pe.wait_ge(s_hi_s, k // 4 + 1)
                    pe.wait_ge(w_hi, W1_CHUNKS + k + 1)
                    pw2_part(0, k)
                if step_k >= PW2_LEAD:
                    k = step_k - PW2_LEAD
                    pw2_part(1, k).then_inc(w_used, 1)

            def keep_clock(count):
                for _ in range(count):
                    nc.tensor.matmul(ps[:, 3, :], ident[:, :], h[:, 0, 0:512], start=True, stop=True)

            pe.wait_ge(rw_s, 16)
            for t in range(TT):
                for k in range(KT):
                    if k % 4 == 0:
                        pe.wait_ge(h_ready, 4 * t + k // 4 + 1)
                    mm = nc.tensor.transpose(ps[:, 4 * t + k // 4, (k % 4) * P:(k % 4 + 1) * P],
                                             h[:, t, k * P:(k + 1) * P], ident[:, :])
                    if k % 8 == 7:
                        mm.then_inc(hT_ps, 1)
                pe.wait_ge(hT_sb[0], 2 + t)
                if t == 1:
                    pe.wait_ge(hT_sb[1], 1)
                for k in range(KT):
                    cg = k % 4
                    mm = nc.tensor.matmul(ps[cg * E:(cg + 1) * E, t, 0:P], rw[:, k * E:(k + 1) * E],
                                          hT[:, k, t * P:(t + 1) * P], start=(k < 4), stop=(k >= KT - 4))
                mm.then_inc(logits, 1)
                pe.wait_ge(logit_sb, t + 1)
                mm = nc.tensor.transpose(ps[:, 2, t * P:(t + 1) * P], logit_parts[:, t * P:(t + 1) * P], ident[:, :])
                if t == 0:
                    keep_clock(4)
            mm.then_inc(logits_T, 1)
            keep_clock(4)
            pe.wait_ge(routed_s, 1)
            nc.tensor.matmul(ps[:, 2, 0:E], before[:, :], routed[:, 0, :], start=True, stop=True)
            nc.tensor.matmul(ps[:, 2, E:2 * E], ones_b[:, :], routed[:, 0, :], start=True, stop=False)
            nc.tensor.matmul(ps[:, 2, E:2 * E], before[:, :], routed[:, 1, :], start=False, stop=True)
            nc.tensor.matmul(ps[:, 3, 0:E], ones_b[:, :], routed[:, 0, :], start=True, stop=False)
            nc.tensor.matmul(ps[:, 3, 0:E], ones_b[:, :], routed[:, 1, :], start=False, stop=True
                             ).then_inc(ranks_ps, 1)

            def gather(p, g):
                pe.wait_ge(picked_s, p + 1)
                dst = (ps_x, ps_add)[g]
                wait(pe, x_sb, 2 * p + g - 1)
                if g == 1:
                    wait(pe, added, 8 * p)
                for c in range(8):
                    for t in range(TT):
                        mm = nc.tensor.matmul(dst[:, c // 4, (c % 4) * P:(c % 4 + 1) * P],
                                              h[:, t, g * 1024 + c:(g + 1) * 1024:8],
                                              pick[:, t, :, :].rearrange("p i s -> p (i s)"),
                                              start=(t == 0), stop=(t == TT - 1))
                mm.then_inc(x_ps, 1)

            def chunk_landed(j, n):
                s = slot_of(j)
                pe.wait_ge(arrived[s], 16 * (landed_before(s) + n) + 16)
                return s

            def pair(i):
                for q in range(2):
                    n = 2 * i + q
                    wait(pe, act_done, n)
                    wait(pe, mid_done, n)
                    for j in range(0, 8, 2):
                        kind, g, c0 = CHUNKS[j]
                        s = chunk_landed(j, n)
                        chunk_landed(j + 1, n)
                        if q == 0 and c0 == 0:
                            pe.wait_ge(x_sb, 2 * i + g + 1)
                        for c in range(4):
                            for hh in range(2):
                                mm = nc.tensor.matmul(
                                    ps_gu[hh * SLOTS:(hh + 1) * SLOTS, :].rearrange("p (a f) -> p a f", a=2),
                                    xgT[:, g * 8 + c0 + c, q, :],
                                    ring[:, s:s + 2, c * FF + hh * 256:c * FF + (hh + 1) * 256],
                                    start=(j == 0 and c == 0), stop=(j == 6 and c == 3))
                        mm.then_inc(freed[s + 1], 1)
                    if q == 0:
                        pe.wait_ge(weighted, i + 1)
                        wait(pe, pT_sb, i)
                        for t in range(TT):
                            mm = nc.tensor.transpose(ps_pT[:, t * P:(t + 1) * P],
                                                     pick_w[:, t, :, :].rearrange("p i s -> p (i s)"), ident[:, :])
                        mm.then_inc(pT_ps, 1)
                    pe.wait_ge(mid_done, n + 1)
                    wait(pe, midT_sb, n)
                    for c in range(2):
                        mm = nc.tensor.transpose(ps_mid[:, c * P:(c + 1) * P], mid[:, c * P:(c + 1) * P], ident[:, :])
                    mm.then_inc(midT_ps, 1)
                    pe.wait_ge(midT_sb, n + 1)
                    wait(pe, y_sb[0], n)
                    wait(pe, y_sb[1], n)
                    for f in range(4):
                        s = chunk_landed(8 + f, n)
                        for nb in range(2):
                            for g in range(2):
                                mm = nc.tensor.matmul(ps_y[g * SLOTS:(g + 1) * SLOTS, nb, :],
                                                      midT[:, f % 2, (f // 2) * SLOTS:(f // 2 + 1) * SLOTS],
                                                      ring[:, s, g * 1024 + nb * 512:g * 1024 + (nb + 1) * 512],
                                                      start=(f == 0), stop=(f == 3))
                        mm.then_inc(freed[s], 1)
                pe.wait_ge(y_sb[0], 2 * i + 2)
                pe.wait_ge(pT_sb, i + 1)
                for t in range(TT):
                    for cb in range(4):
                        k = 4 * t + cb
                        if k == 2:
                            pe.wait_ge(y_sb[1], 2 * i + 2)
                        if k < 2:
                            pe.wait_ge(x_sb, 2 * i + 2)
                        wait(pe, added, 8 * i + k - 1)
                        nc.tensor.matmul(ps_add[:, k % 2, :], pickT[:, t, :], y[:, cb * 512:(cb + 1) * 512],
                                         start=True, stop=True).then_inc(add_ps, 1)
                for g in range(2):
                    gather(i + 1, g)

            for g in range(2):
                gather(0, g)
            more_pairs = load_pairs(pe)
            item_loop(pe, pair, more_pairs)


def kernel(**inputs):
    import numpy as np
    import concourse.bacc as bacc
    from concourse import mybir as _mybir
    from concourse.bass_utils import run_bass_kernel_spmd

    inp = {n: np.asarray(a) for n, a in inputs.items()}
    tokens = np.concatenate([inp["meta_tokens"], inp["x"][0]], axis=0)
    tiles = [inp["conv_pw1_b"][0][:D].reshape(KT, P), inp["conv_pw1_b"][0][D:].reshape(KT, P),
             inp["conv_dw_b"][0].reshape(KT, P), inp["conv_ln_g"][0].reshape(KT, P), inp["conv_ln_b"][0].reshape(KT, P)]
    tiles += [tap.reshape(KT, P) for tap in inp["conv_dw_w"][0]]
    par = np.stack(tiles, axis=0).transpose(2, 1, 0).reshape(P, KT * PAR)
    rw = inp["router_w"].reshape(KT, P, E).transpose(1, 0, 2).reshape(P, KT * E)
    arrays = {
        "xT": tokens.T, "x": inp["x"][0], "par": par, "w1": inp["conv_pw1_w"][0], "w2": inp["conv_pw2_w"][0],
        "b2": inp["conv_pw2_b"], "ln1_g": inp["ln_mix_g"], "ln1_b": inp["ln_mix_b"],
        "ln2_g": inp["ln_ffn_g"], "ln2_b": inp["ln_ffn_b"], "rw": rw, "rb": inp["router_b"].reshape(1, E),
        "wg": inp["moe_w_gate"][0], "wu": inp["moe_w_up"][0], "wd": inp["moe_w_down"][0],
    }
    arrays = {f"in_{n}": np.ascontiguousarray(a) for n, a in arrays.items()}

    nc = bacc.Bacc("TRN2", target_bir_lowering=False, num_devices=1)
    args = [nc.dram_tensor(n, a.shape, _mybir.dt.from_np(a.dtype), kind="ExternalInput").ap()
            for n, a in arrays.items()]
    out = nc.dram_tensor("out", (SEQ, D), _mybir.dt.float32, kind="ExternalOutput").ap()
    build(nc, *args, out)
    result = run_bass_kernel_spmd(nc, [arrays], core_ids=[0])
    return result.results[0]["out"].reshape(1, SEQ, D)
```
